# Optimizing a Trainium2 kernel written in Bass

```python
import jax, jax.numpy as jnp
from jax import lax
import numpy as np

D_MODEL = 2048
BATCH = 1
SEQ = 256
DEPTH = 1

CHUNK = 64
Q_BLOCK = 128
D_PLE = 256
EPS = 1e-6

POOL_WIDTH = D_MODEL // 2
POOL_WINDOWS = (2, 4, 8, 16)
POOL_GROUPS = len(POOL_WINDOWS)
POOL_GROUP_WIDTH = POOL_WIDTH // POOL_GROUPS

V_HEAD = 128
MLA_HEADS = (D_MODEL // 2) // V_HEAD
MLA_WIDTH = MLA_HEADS * V_HEAD
QK_NOPE = 128
QK_ROPE = 64
QK_HEAD = QK_NOPE + QK_ROPE
Q_LORA = 512
KV_LORA = 512
ROPE_THETA = 10000.0

MIX_WIDTH = POOL_WIDTH + MLA_WIDTH
IN_COLS = POOL_WIDTH + Q_LORA + KV_LORA + QK_ROPE

PEER_HEADS = 8
PEER_NKEYS = 128
PEER_EXPERTS = PEER_NKEYS * PEER_NKEYS
PEER_DKEY = 256
PEER_HALF = PEER_DKEY // 2
PEER_TOPK = 16
PEER_TOK_BLOCK = 128


def rms_norm(x, g):
    xf = x.astype(jnp.float32)
    y = xf * lax.rsqrt(jnp.mean(xf * xf, axis=-1, keepdims=True) + EPS)
    return (y * g.astype(jnp.float32)).astype(x.dtype)

def apply_rope(x, cos, sin):
    half = QK_ROPE // 2
    xf = x.astype(jnp.float32)
    x1, x2 = xf[..., :half], xf[..., half:]
    return jnp.concatenate([x1 * cos - x2 * sin, x2 * cos + x1 * sin], axis=-1).astype(x.dtype)

def pool_mixer(xp, w_pool, pool_scale):
    B, S, _ = xp.shape
    xf = xp.reshape(B, S, POOL_GROUPS, POOL_GROUP_WIDTH).astype(jnp.float32)
    cs = jnp.cumsum(xf, axis=1)
    t = jnp.arange(S)
    outs = []
    for g, w in enumerate(POOL_WINDOWS):
        csg = cs[:, :, g]
        lower = jnp.pad(csg, ((0, 0), (w, 0), (0, 0)))[:, :S]
        cnt = jnp.minimum(t + 1, w).astype(jnp.float32)[None, :, None]
        outs.append((csg - lower) / cnt - xf[:, :, g])
    d = jnp.stack(outs, axis=2).astype(xp.dtype)
    y = jnp.einsum('bsgc,gcd->bsgd', d, w_pool)
    return y.reshape(B, S, POOL_WIDTH) * pool_scale

def mla(c_q, c_kv, k_rope, positions, q_lat_gain, kv_lat_gain, w_uq, w_ukv, q_norm_gain, k_norm_gain):
    B, S, _ = c_q.shape
    q = (rms_norm(c_q, q_lat_gain) @ w_uq).reshape(B, S, MLA_HEADS, QK_HEAD)
    kv = (rms_norm(c_kv, kv_lat_gain) @ w_ukv).reshape(B, S, MLA_HEADS, QK_NOPE + V_HEAD)
    k_nope, v = kv[..., :QK_NOPE], kv[..., QK_NOPE:]
    k = jnp.concatenate([k_nope, jnp.broadcast_to(k_rope[:, :, None, :], (B, S, MLA_HEADS, QK_ROPE))], axis=-1)
    q = rms_norm(q, q_norm_gain)
    k = rms_norm(k, k_norm_gain)
    inv_freq = ROPE_THETA ** (-jnp.arange(0, QK_ROPE, 2, dtype=jnp.float32) / QK_ROPE)
    ang = positions.astype(jnp.float32)[:, :, None] * inv_freq
    cos, sin = jnp.cos(ang)[:, :, None, :], jnp.sin(ang)[:, :, None, :]
    q = jnp.concatenate([q[..., :QK_NOPE], apply_rope(q[..., QK_NOPE:], cos, sin)], axis=-1)
    k = jnp.concatenate([k[..., :QK_NOPE], apply_rope(k[..., QK_NOPE:], cos, sin)], axis=-1)

    nb = S // Q_BLOCK
    qb = q.reshape(B, nb, Q_BLOCK, MLA_HEADS, QK_HEAD).transpose(1, 0, 2, 3, 4)
    k_chunk = jnp.arange(S) // CHUNK
    scale = QK_HEAD ** -0.5

    def attend(args):
        q_blk, blk = args
        q_chunk = (blk * Q_BLOCK + jnp.arange(Q_BLOCK)) // CHUNK
        s = jnp.einsum('bqhd,bkhd->bhqk', q_blk, k, preferred_element_type=jnp.float32) * scale
        s = jnp.where(k_chunk[None, :] <= q_chunk[:, None], s, -jnp.inf)
        pr = jax.nn.softmax(s, axis=-1).astype(v.dtype)
        return jnp.einsum('bhqk,bkhd->bqhd', pr, v)

    o = lax.map(attend, (qb, jnp.arange(nb)))
    return o.transpose(1, 0, 2, 3, 4).reshape(B, S, MLA_WIDTH)

def peer(xn, w_pq, sub_k1, sub_k2, expert_u, expert_v):
    B, S, D = xn.shape
    q = (xn @ w_pq).reshape(B, S, PEER_HEADS, 2, PEER_HALF)
    s1 = jnp.einsum('bshd,hnd->bshn', q[..., 0, :], sub_k1, preferred_element_type=jnp.float32)
    s2 = jnp.einsum('bshd,hnd->bshn', q[..., 1, :], sub_k2, preferred_element_type=jnp.float32)
    v1, i1 = lax.top_k(s1, PEER_TOPK)
    v2, i2 = lax.top_k(s2, PEER_TOPK)
    cand = (v1[..., :, None] + v2[..., None, :]).reshape(B, S, PEER_HEADS, PEER_TOPK * PEER_TOPK)
    vs, ci = lax.top_k(cand, PEER_TOPK)
    e1 = jnp.take_along_axis(i1, ci // PEER_TOPK, axis=-1)
    e2 = jnp.take_along_axis(i2, ci % PEER_TOPK, axis=-1)
    eidx = e1 * PEER_NKEYS + e2
    gates = jax.nn.softmax(vs, axis=-1).astype(xn.dtype)

    T = B * S
    nblk = T // PEER_TOK_BLOCK
    kk = PEER_HEADS * PEER_TOPK
    xt = xn.reshape(nblk, PEER_TOK_BLOCK, D)
    it = eidx.reshape(nblk, PEER_TOK_BLOCK, kk)
    gt = gates.reshape(nblk, PEER_TOK_BLOCK, kk)

    def block(args):
        xb, ib, gb = args
        act = jax.nn.gelu(jnp.einsum('tkd,td->tk', expert_u[ib], xb))
        return jnp.einsum('tk,tkd->td', act * gb, expert_v[ib])

    return lax.map(block, (xt, it, gt)).reshape(B, S, D)

def first_inputs(seed: int = 0) -> dict:
    key = jax.random.key(seed)
    ks = jax.random.split(key, 24)
    f32 = jnp.float32

    def nrm(k, shape, scale):
        return jax.random.normal(k, shape, f32) * scale

    def gain(k, n):
        return 1.0 + 0.02 * jax.random.normal(k, (DEPTH, n), f32)

    x = jax.random.normal(ks[0], (BATCH, SEQ, D_MODEL), f32)
    p = jax.random.normal(ks[1], (DEPTH, BATCH, SEQ, D_PLE), f32)
    offs = jax.random.randint(ks[2], (BATCH, 1), 0, 4096, dtype=jnp.int32)
    positions = offs + jnp.arange(SEQ, dtype=jnp.int32)[None, :]
    return {
        "x": x,
        "p": p,
        "positions": positions,
        "mix_norm_gain": gain(ks[3], D_MODEL),
        "w_in": nrm(ks[4], (DEPTH, D_MODEL, IN_COLS), D_MODEL ** -0.5),
        "w_pool": nrm(ks[5], (DEPTH, POOL_GROUPS, POOL_GROUP_WIDTH, POOL_GROUP_WIDTH), POOL_GROUP_WIDTH ** -0.5),
        "pool_scale": 1.0 + 0.1 * jax.random.normal(ks[6], (DEPTH, POOL_WIDTH), f32),
        "q_lat_gain": gain(ks[7], Q_LORA),
        "kv_lat_gain": gain(ks[8], KV_LORA),
        "w_uq": nrm(ks[9], (DEPTH, Q_LORA, MLA_HEADS * QK_HEAD), Q_LORA ** -0.5),
        "w_ukv": nrm(ks[10], (DEPTH, KV_LORA, MLA_HEADS * (QK_NOPE + V_HEAD)), KV_LORA ** -0.5),
        "q_norm_gain": gain(ks[11], QK_HEAD),
        "k_norm_gain": gain(ks[12], QK_HEAD),
        "w_out": nrm(ks[13], (DEPTH, MIX_WIDTH, D_MODEL), MIX_WIDTH ** -0.5),
        "ffn_norm_gain": gain(ks[14], D_MODEL),
        "w_pq": nrm(ks[15], (DEPTH, D_MODEL, PEER_HEADS * PEER_DKEY), D_MODEL ** -0.5),
        "sub_k1": nrm(ks[16], (DEPTH, PEER_HEADS, PEER_NKEYS, PEER_HALF), PEER_HALF ** -0.5),
        "sub_k2": nrm(ks[17], (DEPTH, PEER_HEADS, PEER_NKEYS, PEER_HALF), PEER_HALF ** -0.5),
        "expert_u": nrm(ks[18], (DEPTH, PEER_EXPERTS, D_MODEL), D_MODEL ** -0.5),
        "expert_v": nrm(ks[19], (DEPTH, PEER_EXPERTS, D_MODEL), PEER_HEADS ** -0.5),
        "ple_norm_gain": gain(ks[20], D_MODEL),
        "w_ple_gate": nrm(ks[21], (DEPTH, D_MODEL, D_MODEL), D_MODEL ** -0.5),
        "w_ple_proj": nrm(ks[22], (DEPTH, D_PLE, D_MODEL), D_PLE ** -0.5),
    }

def first_block(x, p, positions, mix_norm_gain, w_in, w_pool, pool_scale, q_lat_gain, kv_lat_gain,
              w_uq, w_ukv, q_norm_gain, k_norm_gain, w_out, ffn_norm_gain, w_pq, sub_k1, sub_k2,
              expert_u, expert_v, ple_norm_gain, w_ple_gate, w_ple_proj):
    h = x
    c0 = POOL_WIDTH
    c1 = c0 + Q_LORA
    c2 = c1 + KV_LORA
    for i in range(DEPTH):
        z = rms_norm(h, mix_norm_gain[i]) @ w_in[i]
        y_pool = pool_mixer(z[..., :c0], w_pool[i], pool_scale[i])
        y_mla = mla(z[..., c0:c1], z[..., c1:c2], z[..., c2:], positions,
                    q_lat_gain[i], kv_lat_gain[i], w_uq[i], w_ukv[i], q_norm_gain[i], k_norm_gain[i])
        h = h + jnp.concatenate([y_pool, y_mla], axis=-1) @ w_out[i]
        h = h + peer(rms_norm(h, ffn_norm_gain[i]), w_pq[i], sub_k1[i], sub_k2[i], expert_u[i], expert_v[i])
        gate = jax.nn.sigmoid(rms_norm(h, ple_norm_gain[i]) @ w_ple_gate[i])
        h = h + gate * (p[i] @ w_ple_proj[i])
    return h


N_ATT_HEADS = 8
HEAD_DIM = 128
ATT_WIDTH = N_ATT_HEADS * HEAD_DIM
MOBA_BLOCK = 256
MOBA_TOPK = 3
Q_CHUNK = 128
N_SGU_GROUPS = 8
SGU_GROUP_DIM = 128
SGU_WIDTH = N_SGU_GROUPS * SGU_GROUP_DIM
SGU_CHUNK = 128
IN_SPLITS = (ATT_WIDTH, ATT_WIDTH, ATT_WIDTH, ATT_WIDTH,
             SGU_WIDTH, SGU_WIDTH, SGU_WIDTH,
             D_MODEL, D_MODEL)
IN_WIDTH = 4 * ATT_WIDTH + 3 * SGU_WIDTH + 2 * D_MODEL
NEG_INF = -1e30


def rms_norm_2(x, g):
    xf = x.astype(jnp.float32)
    y = xf * lax.rsqrt(jnp.mean(xf * xf, axis=-1, keepdims=True) + EPS)
    return (y * g.astype(jnp.float32)).astype(x.dtype)

def moba_attention(q, k, v):
    B, S, H, Dh = q.shape
    nb = -(-S // MOBA_BLOCK)
    s_pad = nb * MOBA_BLOCK
    topk = min(MOBA_TOPK, nb)
    nc = S // Q_CHUNK
    scale = Dh ** -0.5

    qh = q.transpose(0, 2, 1, 3)
    pad = ((0, 0), (0, 0), (0, s_pad - S), (0, 0))
    kh = jnp.pad(k.transpose(0, 2, 1, 3), pad)
    vh = jnp.pad(v.transpose(0, 2, 1, 3), pad)
    k_blocks = kh.reshape(B, H, nb, MOBA_BLOCK, Dh)
    v_blocks = vh.reshape(B, H, nb, MOBA_BLOCK, Dh)
    k_mean = jnp.mean(k_blocks.astype(jnp.float32), axis=3)
    q_chunks = qh.reshape(B, H, nc, Q_CHUNK, Dh).transpose(2, 0, 1, 3, 4)

    bi = jnp.arange(B)[:, None, None, None]
    hi = jnp.arange(H)[None, :, None, None]
    blk_ids = jnp.arange(nb)

    def one_chunk(args):
        qc, c = args
        q_pos = c * Q_CHUNK + jnp.arange(Q_CHUNK)
        cur = (c * Q_CHUNK) // MOBA_BLOCK
        gate = jnp.einsum('bhqd,bhnd->bhqn', qc.astype(jnp.float32), k_mean)
        gate = jnp.where(blk_ids < cur, gate, NEG_INF)
        _, idx = lax.top_k(gate, topk)
        valid = idx < cur
        k_sel = k_blocks[bi, hi, idx]
        v_sel = v_blocks[bi, hi, idx]
        s_past = jnp.einsum('bhqd,bhqknd->bhqkn', qc, k_sel,
                            preferred_element_type=jnp.float32) * scale
        s_past = jnp.where(valid[..., None], s_past, NEG_INF)
        k_own = lax.dynamic_index_in_dim(k_blocks, cur, axis=2, keepdims=False)
        v_own = lax.dynamic_index_in_dim(v_blocks, cur, axis=2, keepdims=False)
        s_own = jnp.einsum('bhqd,bhnd->bhqn', qc, k_own,
                           preferred_element_type=jnp.float32) * scale
        key_pos = cur * MOBA_BLOCK + jnp.arange(MOBA_BLOCK)
        s_own = jnp.where(key_pos[None, :] <= q_pos[:, None], s_own, NEG_INF)
        logits = jnp.concatenate(
            [s_past.reshape(B, H, Q_CHUNK, topk * MOBA_BLOCK), s_own], axis=-1)
        p = jax.nn.softmax(logits, axis=-1)
        p_past = p[..., :topk * MOBA_BLOCK].reshape(B, H, Q_CHUNK, topk, MOBA_BLOCK)
        p_own = p[..., topk * MOBA_BLOCK:]
        o = (jnp.einsum('bhqkn,bhqknd->bhqd', p_past.astype(v_sel.dtype), v_sel)
             + jnp.einsum('bhqn,bhnd->bhqd', p_own.astype(v_own.dtype), v_own))
        return o.astype(qc.dtype)

    out = lax.map(one_chunk, (q_chunks, jnp.arange(nc, dtype=jnp.int32)))
    return out.transpose(1, 0, 3, 2, 4).reshape(B, S, H * Dh)

def spatial_gating(u, v, v_norm_g, w_s, b_s):
    B, S, _ = u.shape
    n = S // SGU_CHUNK
    vg = rms_norm_2(v.reshape(B, S, N_SGU_GROUPS, SGU_GROUP_DIM), v_norm_g)
    vg = vg.reshape(B, n, SGU_CHUNK, N_SGU_GROUPS, SGU_GROUP_DIM)
    causal = jnp.tril(jnp.ones((SGU_CHUNK, SGU_CHUNK), dtype=bool))
    w = jnp.where(causal[None], w_s, jnp.zeros((), w_s.dtype))
    mixed = jnp.einsum('gts,bnsgc->bntgc', w, vg) + b_s.T[:, :, None]
    return u * mixed.reshape(B, S, SGU_WIDTH)

def hybrid_layer(x, norm_g, w_in, q_norm_g, k_norm_g, sgu_norm_g, w_s, b_s,
                 w_proj_a, w_proj_b, w_out):
    B, S, _ = x.shape
    h = rms_norm_2(x, norm_g)
    proj = h @ w_in
    cuts = [int(c) for c in np.cumsum(IN_SPLITS)[:-1]]
    q, k, v, z_a, u_b, v_b, z_b, g_a, g_b = jnp.split(proj, cuts, axis=-1)
    q = rms_norm_2(q.reshape(B, S, N_ATT_HEADS, HEAD_DIM), q_norm_g)
    k = rms_norm_2(k.reshape(B, S, N_ATT_HEADS, HEAD_DIM), k_norm_g)
    v = v.reshape(B, S, N_ATT_HEADS, HEAD_DIM)
    att = moba_attention(q, k, v)
    y_a = (att * jax.nn.silu(z_a)) @ w_proj_a
    sgu = spatial_gating(jax.nn.gelu(u_b), jax.nn.gelu(v_b), sgu_norm_g, w_s, b_s)
    y_b = (sgu * jax.nn.silu(z_b)) @ w_proj_b
    merged = jax.nn.sigmoid(g_a) * y_a + jax.nn.sigmoid(g_b) * y_b
    return x + merged @ w_out

def second_inputs(seed: int = 0) -> dict:
    key = jax.random.key(seed)
    ks = jax.random.split(key, 12)
    f32 = jnp.float32
    x = jax.random.normal(ks[0], (BATCH, SEQ, D_MODEL), f32)
    norm_g = 1.0 + 0.02 * jax.random.normal(ks[1], (DEPTH, D_MODEL), f32)
    w_in = jax.random.normal(ks[2], (DEPTH, D_MODEL, IN_WIDTH), f32) * D_MODEL ** -0.5
    q_norm_g = 1.0 + 0.02 * jax.random.normal(ks[3], (DEPTH, HEAD_DIM), f32)
    k_norm_g = 1.0 + 0.02 * jax.random.normal(ks[4], (DEPTH, HEAD_DIM), f32)
    sgu_norm_g = 1.0 + 0.02 * jax.random.normal(ks[5], (DEPTH, SGU_GROUP_DIM), f32)
    w_spatial = jax.random.normal(ks[6], (DEPTH, N_SGU_GROUPS, SGU_CHUNK, SGU_CHUNK), f32) * SGU_CHUNK ** -0.5
    b_spatial = 1.0 + 0.1 * jax.random.normal(ks[7], (DEPTH, N_SGU_GROUPS, SGU_CHUNK), f32)
    w_proj_a = jax.random.normal(ks[8], (DEPTH, ATT_WIDTH, D_MODEL), f32) * ATT_WIDTH ** -0.5
    w_proj_b = jax.random.normal(ks[9], (DEPTH, SGU_WIDTH, D_MODEL), f32) * SGU_WIDTH ** -0.5
    w_out = jax.random.normal(ks[10], (DEPTH, D_MODEL, D_MODEL), f32) * D_MODEL ** -0.5
    return {"x": x, "norm_g": norm_g, "w_in": w_in, "q_norm_g": q_norm_g,
            "k_norm_g": k_norm_g, "sgu_norm_g": sgu_norm_g, "w_spatial": w_spatial,
            "b_spatial": b_spatial, "w_proj_a": w_proj_a, "w_proj_b": w_proj_b,
            "w_out": w_out}

def second_block(x, norm_g, w_in, q_norm_g, k_norm_g, sgu_norm_g, w_spatial, b_spatial,
              w_proj_a, w_proj_b, w_out):
    for l in range(DEPTH):
        x = hybrid_layer(x, norm_g[l], w_in[l], q_norm_g[l], k_norm_g[l], sgu_norm_g[l],
                         w_spatial[l], b_spatial[l], w_proj_a[l], w_proj_b[l], w_out[l])
    return x


def setup_inputs(seed=0):
    out = dict(first_inputs(seed))
    for name, value in second_inputs(seed + 1).items():
        if name != "x":
            out[name + "_2"] = value
    return out


def reference(
    x, p, positions, mix_norm_gain, w_in, w_pool, pool_scale, q_lat_gain, kv_lat_gain, w_uq,
    w_ukv, q_norm_gain, k_norm_gain, w_out, ffn_norm_gain, w_pq, sub_k1, sub_k2, expert_u,
    expert_v, ple_norm_gain, w_ple_gate, w_ple_proj, norm_g_2, w_in_2, q_norm_g_2, k_norm_g_2,
    sgu_norm_g_2, w_spatial_2, b_spatial_2, w_proj_a_2, w_proj_b_2, w_out_2,
):
    x = first_block(
        x, p, positions, mix_norm_gain, w_in, w_pool, pool_scale, q_lat_gain, kv_lat_gain, w_uq,
        w_ukv, q_norm_gain, k_norm_gain, w_out, ffn_norm_gain, w_pq, sub_k1, sub_k2, expert_u,
        expert_v, ple_norm_gain, w_ple_gate, w_ple_proj,
    )
    return second_block(
        x, norm_g_2, w_in_2, q_norm_g_2, k_norm_g_2, sgu_norm_g_2, w_spatial_2, b_spatial_2,
        w_proj_a_2, w_proj_b_2, w_out_2,
    )


_drawn_inputs = setup_inputs


def setup_inputs(seed=0):
    import zlib

    import numpy as np

    out = dict(_drawn_inputs(seed))
    spreads = {}
    factors = {'mix_norm_gain': 3.028,
     'q_lat_gain': 8.0,
     'kv_lat_gain': 6.671,
     'q_norm_gain': 8.0,
     'k_norm_gain': 7.377,
     'ple_norm_gain': 193.078,
     'norm_g_2': 8.0,
     'q_norm_g_2': 34.932,
     'k_norm_g_2': 90.876,
     'sgu_norm_g_2': 24.292,
     'b_spatial_2': 9.861,
     'ffn_norm_gain': 4.114}
    for name, (base, spread) in spreads.items():
        noise = np.random.default_rng([zlib.crc32(name.encode()), seed]).standard_normal(out[name].shape)
        drawn = base * np.exp(spread * noise) if base else spread * noise
        out[name] = __import__('jax').numpy.asarray(drawn.astype(out[name].dtype))
    for name, factor in factors.items():
        out[name] = (out[name] * factor).astype(out[name].dtype)
    return out
```

```python
from contextlib import ExitStack, contextmanager

import numpy as np
import concourse.bass as bass
from concourse import mybir

F32, F32R = mybir.dt.float32, mybir.dt.float32r
I32, U32 = mybir.dt.int32, mybir.dt.uint32
ALU, ACT = mybir.AluOpType, mybir.ActivationFunctionType
AX = mybir.AxisListType.X
ENG = mybir.EngineType

P128 = 128
S = 256
NT = S // P128
D = 2048
DK = D // P128
EPS = 1e-6
POOL_W, POOL_WINDOWS = 1024, (2, 4, 8, 16)
NH, QN, QR, LORA = 8, 128, 64, 512
QH = QN + QR
CHUNK = 64
TOPK, NKEYS, EXPERTS = 16, 128, 16384
PLE = 256
AW = 1024
CW = 2048
NC = 512
RAW = 4
SPL = 2
GR = 8
NEG = -1e30

N_CHUNKS = dict(w_in=16, w_rope=1, w_pool=1, w_uq=3, w_ukv=4, w_out=16, w_pq=16, sub_k=1, ple_proj=2, ple_gate=16,
                w_in_2=56, merge=48, w_out_2=16)
CHUNKS = sum(N_CHUNKS.values())

COLS, _at = {}, 0
for _n, _w in (("mix", 16), ("ple", 16), ("norm2", 16), ("pool_scale", 8), ("q_lat", 4), ("kv_lat", 4),
               ("b_spatial", 8)):
    COLS[_n] = _at
    _at += _w
N_COLS = _at
ROWS, _at = {}, 0
for _n, _w in (("q_norm", QH), ("k_norm", QH), ("q_norm2", 128), ("k_norm2", 128), ("sgu", 128), ("inv_freq", 32),
               ("iota", 16)):
    ROWS[_n] = _at
    _at += _w
N_ROWS = _at


class Mark:
    def __init__(self, sem, const, per=0, i=None):
        self.sem, self.const, self.per, self.i = sem, const, per, i

    def value(self):
        return self.const if self.i is None or not self.per else self.i * self.per + self.const


class Counter:
    def __init__(self, sem, count=0):
        self.sem, self.count, self.start, self.per, self.i = sem, count, count, 0, None

    def mark(self, back=0):
        return Mark(self.sem, self.count - back, self.per, self.i)


class Lane:
    def __init__(self, eng, sem, chained=True):
        self.eng, self.own, self.chained, self.last = eng, Counter(sem), chained, []
        self.counters = [self.own]

    def after(self, *marks):
        for m in list(marks) + (self.last if self.chained else []):
            self.eng.wait_ge(m.sem, m.value())
        return self.eng

    def done(self, ins, counter=None):
        c = counter or self.own
        ins.then_inc(c.sem, 1)
        c.count += 1
        self.last = [c.mark()]
        return c.mark()

    def mark(self):
        return self.own.mark()


def build(nc, x, cols, rows, positions, ffn_gain, pool_op, p_t, w_spatial_t, weights, expert_u, expert_v, out):
    with ExitStack() as ctx:
        def sb(name, shape, dt=F32):
            return ctx.enter_context(nc.sbuf_tensor(name, shape, dt))

        def sem(name):
            return ctx.enter_context(nc.semaphore(name))

        def placed():
            return -(-nc.sbuf_base // 32) * 32

        def over(name, base, at, shape, dt=F32R):
            return nc.alloc_sbuf_tensor_at(name, [128] + shape, dt, offset=base + 4 * at)

        raw = sb("raw", [128, RAW, CW])
        whi = sb("whi", [128, SPL, CW], F32R)
        wlo = sb("wlo", [128, SPL, CW], F32R)
        xT_at = placed()
        xT = sb("xT", [128, 2, DK * S], F32R)
        h = sb("h", [128, NT, D])
        W_at = placed()
        W = sb("W", [128, 20736])
        colv = sb("colv", [128, N_COLS])
        rowv = sb("rowv", [128, N_ROWS])
        ident = sb("ident", [128, 128])
        mask = sb("mask", [128, 2, 256])
        tmp = sb("tmp", [128, 1024])
        pos = sb("pos", [128, NT], I32)
        trig = sb("trig", [128, 2, NT, 32])
        st = sb("st", [128, 96])
        idx = sb("idx", [128, NT, 128], I32)
        gate = sb("gate", [128, NT, 128])
        act = sb("act", [128, NT, 128])
        idx_now = sb("idx_now", [128, 16], I32)
        col_now = sb("col_now", [128, 16])
        ps = ctx.enter_context(nc.psum_tensor("ps", [128, 8, 512], F32))

        xh = xT[:, 0, :].rearrange("p (k s) -> p k s", k=DK)
        xl = xT[:, 1, :].rearrange("p (k s) -> p k s", k=DK)

        def w(at, *shape):
            n = int(np.prod(shape))
            v = W[:, at:at + n]
            if len(shape) == 2:
                v = v.rearrange("p (a b) -> p a b", a=shape[0])
            elif len(shape) == 3:
                v = v.rearrange("p (a b c) -> p a b c", a=shape[0], b=shape[1])
            return v

        def row(name, n):
            return rowv[:, ROWS[name]:ROWS[name] + n]

        V = Lane(nc.vector, sem("v_done"))
        A = Lane(nc.scalar, sem("a_done"))
        T = Lane(nc.tensor, sem("t_done"), chained=False)
        G = Lane(nc.gpsimd, sem("p_done"))
        hi_done = Counter(sem("hi_done"))
        lo_done = Counter(sem("lo_done"))
        used = Counter(sem("used"))
        evac = Counter(sem("evac"))
        rows_used = Counter(sem("rows_used"), GR)
        A.counters += [hi_done, evac]
        V.counters += [lo_done, evac, rows_used]
        T.counters += [used]
        landed = [sem(f"landed{r}") for r in range(RAW)]
        row_in = [sem(f"row_in{r}") for r in range(GR)]
        loads = {n: sem("load_" + n) for n in ("x", "cols", "rows", "pos", "pool_op", "p", "ffn", "ws", "out")}
        everything = [V.own, A.own, T.own, G.own, hi_done, lo_done, used, evac, rows_used]

        @contextmanager
        def loop(n, per, lanes):
            base = {c: c.count for c in everything}
            with nc.Fori(0, n, engines=[{V: ENG.DVE, A: ENG.Activation, T: ENG.PE, G: ENG.Pool}[k] for k in lanes]) as i:
                for c, k in per.items():
                    c.per, c.i = k, i
                for k in lanes:
                    k.last = [c.mark() for c in k.counters if c.count != c.start or c in per]
                yield i
                got = {c: c.count - base[c] for c in everything if c.count != base[c]}
                assert got == per, sorted((c.sem.name, v) for c, v in got.items())
            for c, k in per.items():
                c.per, c.i, c.count = 0, None, base[c] + k * n
            for k in lanes:
                k.last = [c.mark() for c in k.counters if c.count != c.start or c in per]

        def load(name, dst, src, *marks):
            for m in marks:
                nc.scalar.wait_ge(m.sem, m.value())
            nc.scalar.dma_start(dst, src).then_inc(loads[name], 16)
            return Mark(loads[name], 16)

        for c in range(RAW):
            nc.sync.dma_start(raw[:, c, :], weights[c]).then_inc(landed[c], 16)
        assert CHUNKS % RAW == 0
        with nc.Fori(0, CHUNKS // RAW - 1, engines=[ENG.SP]) as g:
            for r in range(RAW):
                nc.sync.wait_ge(used.sem, g * RAW + (r + 1))
                nc.sync.dma_start(raw[:, r, :], weights[bass.ds(g * RAW + (RAW + r), 1)].rearrange("a p n -> p (a n)"))\
                    .then_inc(landed[r], 16)

        for t in range(NT):
            nc.scalar.dma_start(h[:, t, :], x[t * 128:(t + 1) * 128, :]).then_inc(loads["x"], 16)
        x_in = Mark(loads["x"], 16 * NT)
        cols_in = load("cols", colv[:, :], cols)
        rows_in = load("rows", rowv[:, :], rows.broadcast_to([128, N_ROWS]))
        pos_in = load("pos", pos[:, :], positions)
        POOL_OP = w(15488, 2, 4, 256)
        pool_in = load("pool_op", W[:, 15488:15488 + 2048], pool_op)

        G.done(G.after().memset(tmp[:, 0:128], 1.0))
        ident_ok = G.done(G.after().affine_select(out=ident[:, :], in_=tmp[:, 0:128], compare_op=ALU.is_equal, fill=0.0,
                                                  base=0, pattern=[[-1, 128]], channel_multiplier=1))
        G.done(G.after().memset(mask[:, :, :], 0.0))
        G.done(G.after().memset(mask[0:CHUNK, 0, 128 + CHUNK:256], NEG))
        mask_ok = G.done(G.after().affine_select(out=mask[:, 1, 128:256], in_=mask[:, 1, 128:256], compare_op=ALU.is_ge,
                                                 fill=NEG, base=0, pattern=[[-1, 128]], channel_multiplier=1))
        T.after(ident_ok)
        V.after(cols_in, rows_in)
        A.after(cols_in)

        split_at = [0]

        def split_next(A=A, V=V):
            c = split_at[0]
            r, b = c % RAW, c % SPL
            per = hi_done.per
            here = Mark(landed[r], 16 * (c // RAW + 1), 16 * per // RAW if per else 0, hi_done.i)
            free = [Mark(used.sem, c - SPL + 1, per, hi_done.i)] if c >= SPL else []
            hi = A.done(A.after(here, *free).activation(whi[:, b, :], raw[:, r, :], ACT.Copy), hi_done)
            V.done(V.after(hi).tensor_tensor(wlo[:, b, :], raw[:, r, :], whi[:, b, :].bitcast(F32), ALU.subtract), lo_done)
            split_at[0] += 1

        def next_chunk(last=False):
            c = used.count
            if not last:
                split_next()
            T.after(Mark(lo_done.sem, c + 1, used.per, used.i))
            return whi[:, c % SPL, :], wlo[:, c % SPL, :]

        def enter(n_chunks):
            pass

        def products(out_ap, a, b, start, stop):
            T.eng.matmul(out_ap, a[0], b[0], start=start, stop=False)
            T.eng.matmul(out_ap, a[0], b[1], start=False, stop=False)
            return T.eng.matmul(out_ap, a[1], b[0], start=False, stop=stop)

        pairs = [0]

        def dense(n_q, evacuate, q0=0, cols_n=NC, lhs=None, last=False, per=0, i=None):
            lh, ll = lhs or (xh, xl)
            pair = 2 * (pairs[0] % 2)
            if pairs[0] >= 2:
                T.after(Mark(evac.sem, pairs[0] - 1, evac.per, evac.i))
            for q in range(n_q):
                hi, lo = next_chunk(last=last and q == n_q - 1)
                nk = min(CW // cols_n, 4 if cols_n == NC else DK)
                for k in range(nk):
                    for t in range(NT):
                        o = ps[:, pair + t, 0:cols_n]
                        s = slice(t * 128, (t + 1) * 128)
                        cs = slice(k * cols_n, (k + 1) * cols_n)
                        ks = q0 + q * 4 + k
                        m = products(o, (lh[:, ks, s], ll[:, ks, s]), (hi[:, cs], lo[:, cs]),
                                     start=(q == 0 and k == 0), stop=(q == n_q - 1 and k == nk - 1))
                got = T.done(m, used)
            pairs[0] += 1
            evacuate([ps[:, pair + t, 0:cols_n] for t in range(NT)], got)

        def dense_loop(n, body, chunks, blocks, per):
            assert chunks % RAW == 0 and blocks % 2 == 0
            c0, p0 = split_at[0], pairs[0]
            full = {hi_done: chunks, lo_done: chunks, used: chunks, evac: blocks}
            full.update(per)
            with loop(n, full, [V, A, T]) as i:
                body(i)
            split_at[0], pairs[0] = c0 + n * chunks, p0 + n * blocks

        def copy_out(dst):
            def f(banks, got):
                V.done(V.after(got).tensor_copy(dst(0), banks[0]))
                V.done(V.after().tensor_copy(dst(1), banks[1]), evac)
            return f

        bank_free = {b: [] for b in range(8)}

        def transposes(n, src, put, *marks, wide=None):
            T.after(*marks)
            for g in range(n // 2):
                b = 4 + g % 2
                T.after(*bank_free[b])
                for k in range(2):
                    for t in range(NT):
                        m = T.eng.transpose(ps[:, b, (2 * k + t) * 128:(2 * k + t + 1) * 128], src(t, 2 * g + k), ident[:, :])
                bank_free[b] = put(g, ps[:, b, :], T.done(m))

        def two(ap, g):
            return ap[:, 2 * g:2 * g + 2, :].rearrange("p k s -> p (k s)")

        def to_split(hi, lo, gain=None):
            def put(g, bank, got):
                if gain is None:
                    m = A.done(A.after(got).activation(two(hi, g), bank, ACT.Copy))
                    m = V.done(V.after(m).tensor_tensor(two(lo, g), bank, two(hi, g).bitcast(F32), ALU.subtract))
                else:
                    s = [colv[:, gain + 2 * g + k:gain + 2 * g + k + 1] for k in range(2)]
                    for k in range(2):
                        m = A.done(A.after(got).activation(hi[:, 2 * g + k, :], bank[:, k * S:(k + 1) * S], ACT.Copy, scale=s[k]))
                    for k in range(2):
                        m = V.done(V.after(m).scalar_tensor_tensor(lo[:, 2 * g + k, :], bank[:, k * S:(k + 1) * S], s[k],
                                                                   hi[:, 2 * g + k, :].bitcast(F32), ALU.mult, ALU.subtract))
                return [m]
            return put

        def to_plain(dst):
            def put(g, bank, got):
                if g % 2:
                    return [A.done(A.after(got).activation(dst[:, g * 512:(g + 1) * 512], bank, ACT.Copy))]
                return [V.done(V.after(got).tensor_copy(dst[:, g * 512:(g + 1) * 512], bank))]
            return put

        def rstd(ss, n, *marks):
            m = V.done(V.after(*marks).tensor_scalar(ss, ss, 1.0 / n, EPS, ALU.mult, ALU.add))
            m = A.done(A.after(m).activation(ss, ss, ACT.Sqrt))
            return V.done(V.after(m).reciprocal(ss, ss))

        def norm_rows(dst, gain=None, *marks):
            junk = ps[:, 4:8, :].rearrange("p a b -> p (a b)")
            free = [m for b in range(4, 8) for m in bank_free[b]]
            for t in range(NT):
                m = A.done(A.after(*marks, *free, V.mark(), T.mark(), x_in)
                           .activation(junk, h[:, t, :], ACT.Square, accum_out=st[:, t:t + 1]))
            for b in range(4, 8):
                bank_free[b] = [m]
            rstd(st[:, 0:NT], D, m)
            for t in range(NT):
                if gain is None:
                    m = V.done(V.after().tensor_scalar(dst(t), h[:, t, :], st[:, t:t + 1], None, ALU.mult))
                else:
                    m = V.done(V.after(gain[1]).scalar_tensor_tensor(dst(t), h[:, t, :], st[:, t:t + 1], gain[0], ALU.mult, ALU.mult))
            return m

        def normed_transpose(gain):
            n = w(0, NT, D)
            m = norm_rows(lambda t: n[:, t, :])
            A.after(used.mark())
            transposes(DK, lambda t, k: n[:, t, k * 128:(k + 1) * 128], to_split(xh, xl, gain), m)
            T.after(V.mark())

        normed_transpose(COLS["mix"])
        split_next()
        Z_W = D + QR
        z = w(0, NT, Z_W)

        def z_body(i):
            for j in range(2):
                dense(4, copy_out(lambda t: z[:, t, bass.ds(i * (2 * NC) + j * NC, NC)]))
        V.after(T.mark())
        dense_loop(2, z_body, 8, 2, {V.own: 2})
        dense(1, copy_out(lambda t: z[:, t, D:Z_W]), cols_n=QR)
        z_ok = evac.mark()

        dTh, dTl = over("dTh", W_at, 11392, [8, S]), over("dTl", W_at, 13440, [8, S])
        T.after(z_ok, pool_in)
        for k in range(8):
            b = 6 + k % 2
            T.after(*bank_free[b])
            for t in range(NT):
                m = T.eng.matmul(ps[:, b, 0:S], z[:, t, k * 128:(k + 1) * 128], POOL_OP[:, t, k // 2, :], start=(t == 0), stop=(t == 1))
            m = A.done(A.after(T.done(m)).activation(dTh[:, k, :], ps[:, b, 0:S], ACT.Copy))
            bank_free[b] = [V.done(V.after(m).tensor_tensor(dTl[:, k, :], ps[:, b, 0:S], dTh[:, k, :].bitcast(F32), ALU.subtract))]

        for j in range(2):
            for t in range(NT):
                c = POOL_W + j * LORA
                m = A.done(A.after(z_ok, ident_ok).activation(tmp[:, 0:LORA], z[:, t, c:c + LORA], ACT.Square, accum_out=st[:, 4 + 2 * j + t:5 + 2 * j + t]))
        rstd(st[:, 4:8], LORA, m)
        for j in range(2):
            for t in range(NT):
                c = POOL_W + j * LORA
                m = V.done(V.after().tensor_scalar(z[:, t, c:c + LORA], z[:, t, c:c + LORA], st[:, 4 + 2 * j + t:5 + 2 * j + t], None, ALU.mult))
        A.after(used.mark())
        transposes(8, lambda t, k: z[:, t, POOL_W + k * 128:POOL_W + (k + 1) * 128],
                   to_split(xh[:, 8:16, :], xl[:, 8:16, :], COLS["q_lat"]), m)

        phi, plo = next_chunk()
        for k in range(8):
            b = 6 + k % 2
            g, half = k // 2, k % 2
            T.after(*bank_free[b], *([V.mark()] if k == 0 else []))
            for c in range(2):
                col = (g * 2 + c) * 256 + half * 128
                m = products(ps[:, b, 0:S], (phi[:, col:col + 128], plo[:, col:col + 128]), (dTh[:, 2 * g + c, :], dTl[:, 2 * g + c, :]),
                             start=(c == 0), stop=(c == 1))
            m = T.done(m, used if k == 7 else None)
            s = colv[:, COLS["pool_scale"] + k:COLS["pool_scale"] + k + 1]
            m = A.done(A.after(m).activation(xh[:, k, :], ps[:, b, 0:S], ACT.Copy, scale=s))
            bank_free[b] = [V.done(V.after(m).scalar_tensor_tensor(xl[:, k, :], ps[:, b, 0:S], s, xh[:, k, :].bitcast(F32), ALU.mult, ALU.subtract))]

        q = w(4224, NT, NH * QH)
        kv = w(7296, NT, NH * 256)
        T.after(V.mark())
        for n in range(3):
            dense(1, copy_out(lambda t: q[:, t, n * NC:(n + 1) * NC]), q0=8)
        for n in range(4):
            dense(1, copy_out(lambda t: kv[:, t, n * NC:(n + 1) * NC]), q0=12)

        TWO_PI = 2 * np.pi
        C1 = 6.28125
        C2 = float(np.float32(np.round((TWO_PI - C1) * 2 ** 19) / 2 ** 19))
        C3 = float(TWO_PI - C1 - C2)
        ang, turns = tmp[:, 0:64].rearrange("p (t f) -> p t f", t=NT), tmp[:, 64:128].rearrange("p (t f) -> p t f", t=NT)
        V.done(V.after(pos_in, A.mark()).tensor_copy(st[:, 8:8 + NT], pos[:, :]))
        for t in range(NT):
            V.done(V.after().tensor_scalar(ang[:, t, :], row("inv_freq", 32), st[:, 8 + t:9 + t], None, ALU.mult))
        V.done(V.after().tensor_scalar(turns, ang, 1.0 / TWO_PI, 12582912.0, ALU.mult, ALU.add))
        V.done(V.after().tensor_scalar(turns, turns, 12582912.0, None, ALU.subtract))
        for c in (C1, C2, C3):
            V.done(V.after().scalar_tensor_tensor(ang, turns, -c, ang, ALU.mult, ALU.add))
        V.done(V.after().tensor_scalar(trig[:, 1, :, :], ang, 3.1415925, -3.1415925, ALU.min, ALU.max))
        V.done(V.after().tensor_scalar(ang, ang, float(np.pi / 2), None, ALU.add))
        V.done(V.after().tensor_scalar(turns, ang, float(np.pi), -TWO_PI, ALU.is_gt, ALU.mult))
        V.done(V.after().tensor_tensor(ang, ang, turns, ALU.add))
        m = V.done(V.after().tensor_scalar(trig[:, 0, :, :], ang, 3.1415925, -3.1415925, ALU.min, ALU.max))
        trig_ok = A.done(A.after(m).activation(trig[:, :, :, :], trig[:, :, :, :], ACT.Sin))

        def heads(ap, n):
            return ap.rearrange("p (h d) -> p h d", h=n)

        def per_head(ap, n, d):
            return ap.unsqueeze(2).broadcast_to([128, n, d])

        def per_dim(ap, n, d):
            return ap.unsqueeze(1).broadcast_to([128, n, d])

        junk = ps[:, 4:8, :].rearrange("p a b -> p (a b)")

        def junk_free():
            return [m for b in range(4, 8) for m in bank_free[b]]

        def set_junk(m):
            for b in range(4, 8):
                bank_free[b] = [m]

        qrh = w(18560, NT, NH * QR)
        krh = w(19584, NT, NH * QR)
        rot_a = tmp[:, 256:512]
        rot_b = tmp[:, 512:768]

        def rotate(dst, src, t, n):
            half = QR // 2
            cos, sin = per_dim(trig[:, 0, t, :], n, half), per_dim(trig[:, 1, t, :], n, half)
            a, b = heads(rot_a[:, 0:n * half], n), heads(rot_b[:, 0:n * half], n)
            x1, x2 = src[:, :, 0:half], src[:, :, half:QR]
            for o, (u, v_), op in ((dst[:, :, 0:half], (x1, x2), ALU.subtract), (dst[:, :, half:QR], (x2, x1), ALU.add)):
                V.done(V.after(trig_ok).tensor_tensor(a, u, cos, ALU.mult))
                V.done(V.after().tensor_tensor(b, v_, sin, ALU.mult))
                m = V.done(V.after().tensor_tensor(o, a, b, op))
            return m

        for t in range(NT):
            qt = heads(q[:, t, :], NH)
            m = A.done(A.after(evac.mark(), *junk_free()).activation(junk[:, 0:NH * QH], q[:, t, :], ACT.Square))
            ss = st[:, 16:24]
            m = V.done(V.after(m).tensor_reduce(ss, heads(junk[:, 0:NH * QH], NH), AX, ALU.add))
            set_junk(m)
            rstd(ss, QH)
            V.done(V.after().tensor_tensor(qt, qt, per_head(ss, NH, QH), ALU.mult))
            V.done(V.after().tensor_tensor(qt, qt, per_dim(row("q_norm", QH), NH, QH), ALU.mult))
            rotate(heads(qrh[:, t, :], NH), qt[:, :, QN:QH], t, NH)
            kt = heads(kv[:, t, :], NH)
            kr = z[:, t, D:Z_W]
            m = A.done(A.after(evac.mark(), *junk_free()).activation(junk, kv[:, t, :], ACT.Square))
            m2 = A.done(A.after(V.mark()).activation(tmp[:, 768:768 + QR], kr, ACT.Square, accum_out=st[:, 32:33]))
            ss = st[:, 24:32]
            m = V.done(V.after(m, m2).tensor_reduce(ss, heads(junk, NH)[:, :, 0:QN], AX, ALU.add))
            set_junk(m)
            V.done(V.after().tensor_scalar(ss, ss, st[:, 32:33], None, ALU.add))
            rstd(ss, QH)
            V.done(V.after().tensor_tensor(kt[:, :, 0:QN], kt[:, :, 0:QN], per_head(ss, NH, QN), ALU.mult))
            V.done(V.after().tensor_tensor(kt[:, :, 0:QN], kt[:, :, 0:QN], per_dim(row("k_norm", QH)[:, 0:QN], NH, QN), ALU.mult))
            kg, kr2 = tmp[:, 128:192], tmp[:, 192:256]
            V.done(V.after().tensor_tensor(kg, kr, row("k_norm", QH)[:, QN:QH], ALU.mult))
            rotate(kr2.unsqueeze(1), kg.unsqueeze(1), t, 1)
            V.done(V.after().tensor_tensor(heads(krh[:, t, :], NH), per_dim(kr2, NH, QR), per_head(ss, NH, QR), ALU.mult))

        qT, qrT = W[:, 11392:13440], W[:, 13440:14464]
        kT, krT = W[:, 0:2048], W[:, 2048:3072]
        A.after(T.mark(), used.mark())
        V.after(T.mark(), used.mark())
        ok = V.mark()
        transposes(NH, lambda t, k: q[:, t, k * QH:k * QH + QN], to_plain(qT), ok)
        transposes(NH, lambda t, k: kv[:, t, k * 256:k * 256 + QN], to_plain(kT), ok)
        transposes(NH // 2, lambda t, k: qrh[:, t, k * 128:(k + 1) * 128], to_plain(qrT), ok)
        transposes(NH // 2, lambda t, k: krh[:, t, k * 128:(k + 1) * 128], to_plain(krT), ok)

        def softmax(n_heads, n_keys, scale, t, score, which, p_out, sums, normed):
            per = 2
            for g in range(n_heads // per):
                b = 6 + g % 2
                T.after(*bank_free[b])
                k = 4 * (g // 2) + g % 2
                for j in range(per):
                    m = score(k + 2 * j, ps[:, b, j * n_keys:(j + 1) * n_keys])
                src = ps[:, b, 0:per * n_keys].rearrange("p (a k) -> p a k", a=per)
                dst = p_out[:, k:k + 3:2, :]
                msk = per_dim(mask[:, which, 256 - n_keys:256], per, n_keys)
                m = V.done(V.after(T.done(m), mask_ok).tensor_tensor(dst, src, msk, ALU.add))
                bank_free[b] = [m]
            mx = st[:, 40:48]
            V.done(V.after().tensor_reduce(mx, p_out, AX, ALU.max))
            nm = V.done(V.after(A.mark()).tensor_scalar(mx, mx, -scale, None, ALU.mult))
            for k in range(n_heads):
                m = A.done(A.after(nm).activation(p_out[:, k, :], p_out[:, k, :], ACT.Exp, bias=mx[:, k:k + 1], scale=scale,
                                                  accum_out=sums[:, k:k + 1]))
            m = V.done(V.after(m).reciprocal(sums, sums))
            if normed:
                m = V.done(V.after().tensor_tensor(p_out, p_out, per_head(sums, n_heads, n_keys), ALU.mult))
            return m

        def turn_probabilities(p_of, dst_of, ok):
            for k in range(NH):
                b = 4 + k % 2
                T.after(ok, *bank_free[b])
                for j, (t, kt_) in enumerate(((0, 0), (1, 0), (1, 1))):
                    m = T.eng.transpose(ps[:, b, j * 128:(j + 1) * 128], p_of(t)[:, k, kt_ * 128:(kt_ + 1) * 128], ident[:, :])
                m = T.done(m)
                if k % 2:
                    bank_free[b] = [V.done(V.after(m).tensor_copy(dst_of(k), ps[:, b, 0:384]))]
                else:
                    bank_free[b] = [A.done(A.after(m).activation(dst_of(k), ps[:, b, 0:384], ACT.Copy))]

        prob = [w(15488, NH, 128), w(16512, NH, 256)]
        pT = w(4224, NH, 384)
        T.after(A.mark(), V.mark())

        def mla_score(t):
            def f(k, o):
                keys, qs = (t + 1) * 128, slice(t * 128, (t + 1) * 128)
                T.eng.matmul(o, qT[:, k * S:(k + 1) * S][:, qs], kT[:, k * S:k * S + keys], start=True, stop=False)
                r = slice(64 * (k % 2), 64 * (k % 2) + 64)
                at = (k // 2) * S
                return T.eng.matmul(o, qrT[r, at:at + S][:, qs], krT[r, at:at + keys], start=False, stop=True)
            return f

        for t in range(NT):
            ok = softmax(NH, (t + 1) * 128, QH ** -0.5, t, mla_score(t), 0, prob[t], st[:, 48:56], True)
        V.after(T.mark())
        A.after(T.mark())
        turn_probabilities(lambda t: prob[t], lambda k: pT[:, k, :], ok)
        T.after(A.mark(), V.mark())
        for g in range(NH // 2):
            b = 6 + g % 2
            T.after(*bank_free[b])
            for j in range(2):
                k = 2 * g + j
                v_of = [kv[:, kt_, k * 256 + QN:(k + 1) * 256] for kt_ in range(2)]
                T.eng.matmul(ps[:, b, j * S:j * S + 128], v_of[0], pT[:, k, 0:128], start=True, stop=True)
                for kt_ in range(2):
                    m = T.eng.matmul(ps[:, b, j * S + 128:(j + 1) * S], v_of[kt_], pT[:, k, 128 + kt_ * 128:256 + kt_ * 128],
                                     start=(kt_ == 0), stop=(kt_ == 1))
            bank_free[b] = to_split(xh[:, 8:16, :], xl[:, 8:16, :])(g, ps[:, b, :], T.done(m))
        T.after(V.mark())

        def residual_body(i):
            for j in range(2):
                def f(banks, got):
                    for t in range(NT):
                        o = h[:, t, bass.ds(i * (2 * NC) + j * NC, NC)]
                        V.done(V.after(got).tensor_tensor(o, banks[t], o, ALU.add), evac if t else None)
                dense(4, f)
        dense_loop(2, residual_body, 8, 2, {V.own: 2})

        xn = w(0, NT, D)
        ffn_row = W[:, 16384:16384 + D]
        ffn_in = load("ffn", ffn_row, ffn_gain.broadcast_to([128, D]), V.mark(), T.mark(), A.mark())
        m = norm_rows(lambda t: xn[:, t, :], (ffn_row, ffn_in), evac.mark())
        A.after(used.mark())
        transposes(DK, lambda t, k: xn[:, t, k * 128:(k + 1) * 128], to_split(xh, xl), m)
        T.after(V.mark())
        qp = w(4096, NT, D)

        def pq_body(i):
            for j in range(2):
                dense(4, copy_out(lambda t: qp[:, t, bass.ds(i * (2 * NC) + j * NC, NC)]))
        dense_loop(2, pq_body, 8, 2, {V.own: 2})
        A.after(used.mark())
        transposes(DK, lambda t, k: qp[:, t, k * 128:(k + 1) * 128], to_split(xh, xl), evac.mark())
        T.after(V.mark(), evac.mark(), *junk_free())
        khi, klo = next_chunk()
        for t in range(NT):
            for k in range(2 * NH):
                s = slice(t * 128, (t + 1) * 128)
                m = products(ps[:, 4 * (1 - t) + k // 4, (k % 4) * 128:(k % 4 + 1) * 128], (xh[:, k, s], xl[:, k, s]),
                             (khi[:, k * 128:(k + 1) * 128], klo[:, k * 128:(k + 1) * 128]), start=True, stop=True)
        m = T.done(m, used)
        sc = w(12288, NT, D)
        for t in range(NT):
            b = 4 * (1 - t)
            m2 = A.done(A.after(m).activation(sc[:, t, :], ps[:, b:b + 4, :].rearrange("p a b -> p (a b)"), ACT.Copy))
            if t == 0:
                set_junk(m2)
            else:
                sc_ok = m2
        proj = w(16384, NT, D)
        pTs = tmp[:, 0:512]
        p_in = load("p", pTs, p_t, V.mark())
        pTh, pTl = over("pTh", W_at, 4096, [2, S]), over("pTl", W_at, 4608, [2, S])
        pTs = pTs.rearrange("p (k s) -> p k s", k=2)
        m = A.done(A.after(p_in, T.mark(), used.mark()).activation(pTh[:, :, :], pTs, ACT.Copy))
        m = V.done(V.after(m).tensor_tensor(pTl[:, :, :], pTs, pTh[:, :, :].bitcast(F32), ALU.subtract))
        T.after(m, sc_ok)
        for c in range(2):
            hi, lo = next_chunk()
            for n in range(2):
                pair = 2 * (pairs[0] % 2)
                T.after(Mark(evac.sem, pairs[0] - 1))
                for t in range(NT):
                    for k in range(2):
                        cs = slice((n * 2 + k) * NC, (n * 2 + k + 1) * NC)
                        m = products(ps[:, pair + t, :], (pTh[:, k, t * 128:(t + 1) * 128], pTl[:, k, t * 128:(t + 1) * 128]),
                                     (hi[:, cs], lo[:, cs]), start=(k == 0), stop=(k == 1))
                m = T.done(m, used if n == 1 else None)
                pairs[0] += 1
                copy_out(lambda t: proj[:, t, (2 * c + n) * NC:(2 * c + n + 1) * NC])(
                    [ps[:, pair + t, :] for t in range(NT)], m)
        proj_done = used.mark()

        best = tmp[:, 0:256].rearrange("p (k n) -> p k n", k=16)
        best_i = tmp[:, 256:512].bitcast(U32).rearrange("p (k n) -> p k n", k=16)
        best_f = tmp[:, 512:768].rearrange("p (k n) -> p k n", k=16)
        top = tmp[:, 768:896].rearrange("p (k n) -> p k n", k=8)
        top_i = tmp[:, 896:1024].bitcast(U32)
        part = [W[:, 5120:5248].bitcast(U32), W[:, 5248:5376].bitcast(U32)]
        part_f = [W[:, 5376:5504], W[:, 5504:5632]]
        e_f = [W[:, 5632:5760], W[:, 5760:5888]]
        cand = W[:, 6144:8192].rearrange("p (k n) -> p k n", k=8)
        hot = W[:, 8192:10240].rearrange("p (k a b) -> p k a b", k=8, a=16)
        V.after(V.mark(), proj_done)

        def top16(vals, out_v, out_i):
            V.done(V.after().max(out_v[:, 0:8], vals))
            V.done(V.after().max_index(out_i[:, 0:8], out_v[:, 0:8], vals))
            V.done(V.after().match_replace(vals, out_v[:, 0:8], vals, -3.0e38))
            V.done(V.after().max(out_v[:, 8:16], vals))
            return V.done(V.after().max_index(out_i[:, 8:16], out_v[:, 8:16], vals))

        for t in range(NT):
            for k in range(2 * NH):
                top16(sc[:, t, k * 128:(k + 1) * 128], best[:, k, :], best_i[:, k, :])
            V.done(V.after().tensor_copy(best_f, best_i))
            pairs4 = best.rearrange("p (h two) n -> p h two n", two=2)
            idx4 = best_f.rearrange("p (h two) n -> p h two n", two=2)
            sums = cand.rearrange("p k (a b) -> p k a b", a=16)
            V.done(V.after().tensor_tensor(sums, pairs4[:, :, 0, :].unsqueeze(3).broadcast_to([128, 8, 16, 16]),
                                           pairs4[:, :, 1, :].unsqueeze(2).broadcast_to([128, 8, 16, 16]), ALU.add))
            for k in range(NH):
                top16(cand[:, k, :], top[:, k, :], top_i[:, k * 16:(k + 1) * 16])
            V.done(V.after().tensor_scalar(part[0], top_i, 4, None, ALU.logical_shift_right))
            V.done(V.after().tensor_scalar(part[1], top_i, 15, None, ALU.bitwise_and))
            for j in range(2):
                V.done(V.after().tensor_copy(part_f[j], part[j]))
                want = part_f[j].rearrange("p (k a) -> p k a", k=8).unsqueeze(3).broadcast_to([128, 8, 16, 16])
                V.done(V.after().tensor_tensor(hot, want, row("iota", 16).unsqueeze(1).unsqueeze(1).broadcast_to([128, 8, 16, 16]), ALU.is_equal))
                V.done(V.after().tensor_tensor(hot, hot, idx4[:, :, j, :].unsqueeze(2).broadcast_to([128, 8, 16, 16]), ALU.mult))
                V.done(V.after().tensor_reduce(e_f[j], hot, AX, ALU.add))
            V.done(V.after().scalar_tensor_tensor(e_f[0], e_f[0], float(NKEYS), e_f[1], ALU.mult, ALU.add))
            V.done(V.after().tensor_copy(idx[:, t, :], e_f[0]))
            g3 = heads(gate[:, t, :], NH)
            m = V.done(V.after().tensor_tensor(g3, top, top[:, :, 0:1].broadcast_to([128, 8, 16]), ALU.subtract))
            m = A.done(A.after(m).activation(gate[:, t, :], gate[:, t, :], ACT.Exp))
            V.done(V.after(m).tensor_reduce(st[:, 56:64], g3, AX, ALU.add))
            V.done(V.after().reciprocal(st[:, 56:64], st[:, 56:64]))
            V.done(V.after().tensor_tensor(g3, g3, per_head(st[:, 56:64], NH, 16), ALU.mult))
        idx_ok = V.mark()

        xT_rows = over("xT_rows", xT_at, 0, [4, D], F32)
        slots = [W[:, 4096 + r * D:4096 + (r + 1) * D] for r in range(4)] + [xT_rows[:, r, :] for r in range(4)]
        G.after(idx_ok, used.mark(), A.mark())
        G.eng.sem_inc(rows_used.sem, GR)
        V.after(idx_ok)

        def peer_pass(t, table, use, n0, v_per):
            with loop(NH, {G.own: 4, V.own: v_per, rows_used: 16}, [G, V]) as i:
                first = rows_used.count - GR
                use(i, None, None, None)
                for j in range(16):
                    r = j % GR
                    free = Mark(rows_used.sem, first + j + 1, 16, i)
                    if j % 4 == 0:
                        ready = G.done(G.after(free).tensor_copy(idx_now[:, j:j + 4], idx[:, t, bass.ds(i * 16 + j, 4)]))
                    for m in (free, ready):
                        G.eng.wait_ge(m.sem, m.value())
                    G.eng.nop(nofuse=True)
                    G.eng.indirect_dma_start(slots[r], None, table[:, :],
                                             bass.IndirectOffsetOnAxis(idx_now[:, j:j + 1], 0)).then_inc(row_in[r], 16)
                    use(i, j, slots[r], Mark(row_in[r], 16 * ((first + j) // GR + 1), 32, i))

        def dot(t):
            def f(i, j, r, m):
                if j is None:
                    return
                V.done(V.after(m).tensor_tensor_reduce(junk, r, xn[:, t, :], 1.0, 0.0, ALU.mult, ALU.add, col_now[:, j:j + 1]), rows_used)
                if j == 15:
                    V.done(V.after().tensor_copy(act[:, t, bass.ds(i * 16, 16)], col_now[:, :]))
            return f

        def add_row(t):
            def f(i, j, r, m):
                if j is None:
                    V.done(V.after().tensor_copy(col_now[:, :], act[:, t, bass.ds(i * 16, 16)]))
                    return
                V.done(V.after(m).scalar_tensor_tensor(h[:, t, :], r, col_now[:, j:j + 1], h[:, t, :], ALU.mult, ALU.add), rows_used)
            return f

        for t in range(NT):
            peer_pass(t, expert_u, dot(t), 0, 1)
            m = A.done(A.after(V.mark()).activation(act[:, t, :], act[:, t, :], ACT.Gelu_apprx_tanh))
            V.done(V.after(m).tensor_tensor(act[:, t, :], act[:, t, :], gate[:, t, :], ALU.mult))
            peer_pass(t, expert_v, add_row(t), 0, 1)
        set_junk(rows_used.mark())

        V.done(V.after().tensor_copy(st[:, 95:96], st[:, 0:1]))
        normed_transpose(COLS["ple"])
        sg = tmp[:, :].rearrange("p (t n) -> p t n", t=NT)

        def ple_body(i):
            for j in range(2):
                def f(banks, got):
                    cs = bass.ds(i * (2 * NC) + j * NC, NC)
                    before = V.mark()
                    for t in range(NT):
                        m = A.done(A.after(got, before).activation(sg[:, t, :], banks[t], ACT.Sigmoid), evac if t else None)
                    for t in range(NT):
                        V.done(V.after(m).tensor_tensor(sg[:, t, :], sg[:, t, :], proj[:, t, cs], ALU.mult))
                        V.done(V.after().tensor_tensor(h[:, t, cs], h[:, t, cs], sg[:, t, :], ALU.add))
                dense(4, f)
        dense_loop(2, ple_body, 8, 2, {V.own: 8, A.own: 2})

        normed_transpose(COLS["norm2"])
        B = w(0, NT, 7 * AW)
        V.after(T.mark())

        def in2_body(i):
            for j in range(2):
                dense(4, copy_out(lambda t: B[:, t, bass.ds(i * (2 * NC) + j * NC, NC)]))
        dense_loop(7, in2_body, 8, 2, {V.own: 2})
        ok = evac.mark()

        def part2(t, s, n=1):
            return B[:, t, s * AW:(s + n) * AW]
        wsT = W[:, 18432:18432 + AW]
        ws_in = load("ws", wsT, w_spatial_t, V.mark())
        ws_ok = G.done(G.after(ws_in).affine_select(out=heads(wsT, 8), in_=heads(wsT, 8), compare_op=ALU.is_ge, fill=0.0,
                                                    base=0, pattern=[[0, 8], [1, 128]], channel_multiplier=-1))

        def norm_groups(ap, gain, ss, *marks):
            m = A.done(A.after(*marks, *junk_free()).activation(junk[:, 0:AW], ap, ACT.Square))
            m = V.done(V.after(m).tensor_reduce(ss, heads(junk[:, 0:AW], 8), AX, ALU.add))
            set_junk(m)
            rstd(ss, 128)
            V.done(V.after().tensor_tensor(heads(ap, 8), heads(ap, 8), per_head(ss, 8, 128), ALU.mult))
            return V.done(V.after().tensor_tensor(heads(ap, 8), heads(ap, 8), per_dim(row(gain, 128), 8, 128), ALU.mult))

        for t in range(NT):
            norm_groups(part2(t, 0), "q_norm2", st[:, 16:24], ok)
            norm_groups(part2(t, 1), "k_norm2", st[:, 24:32])
        for t in range(NT):
            m = A.done(A.after(ok).activation(part2(t, 4, 2), part2(t, 4, 2), ACT.Gelu_apprx_tanh))
        for t in range(NT):
            norm_groups(part2(t, 5), "sgu", st[:, 32:40], m)
        for t in range(NT):
            A.done(A.after().activation(part2(t, 3), part2(t, 3), ACT.Silu))
            silu_ok = A.done(A.after().activation(part2(t, 6), part2(t, 6), ACT.Silu))

        q2T, k2T = W[:, 14336:16384], W[:, 16384:18432]
        ok = V.mark()
        transposes(8, lambda t, k: part2(t, 0)[:, k * 128:(k + 1) * 128], to_plain(q2T), ok)
        transposes(8, lambda t, k: part2(t, 1)[:, k * 128:(k + 1) * 128], to_plain(k2T), ok)
        T.after(A.mark(), V.mark())
        prob2 = [B[:, 0, 0:1024].rearrange("p (k n) -> p k n", k=8), B[:, 1, 0:2048].rearrange("p (k n) -> p k n", k=8)]
        o2 = [part2(0, 0), part2(1, 0)]
        tp = tmp

        def causal_score(t):
            def f(k, o):
                return T.eng.matmul(o, q2T[:, k * S + t * 128:k * S + (t + 1) * 128], k2T[:, k * S:k * S + (t + 1) * 128], start=True, stop=True)
            return f
        V.after(T.mark())
        for t in range(NT):
            ok = softmax(8, (t + 1) * 128, 128 ** -0.5, t, causal_score(t), 1, prob2[t], st[:, 48 + 8 * t:56 + 8 * t], False)
        pT2 = W[:, 14336:14336 + 3072].rearrange("p (k n) -> p k n", k=8)
        A.after(T.mark())
        V.after(T.mark())
        turn_probabilities(lambda t: prob2[t], lambda k: pT2[:, k, :], ok)
        T.after(A.mark(), V.mark())
        for t in range(NT):
            for g in range(2):
                b = 6 + g
                T.after(*bank_free[b])
                for j in range(4):
                    k = 4 * g + j
                    for kt_ in range(t + 1):
                        at = 0 if t == 0 else 128 + kt_ * 128
                        m = T.eng.matmul(ps[:, b, j * 128:(j + 1) * 128], pT2[:, k, at:at + 128], part2(kt_, 2)[:, k * 128:(k + 1) * 128],
                                         start=(kt_ == 0), stop=(kt_ == t))
                m = T.done(m)
                for j in range(4):
                    k = 4 * g + j
                    s = slice(k * 128, (k + 1) * 128)
                    m2 = V.done(V.after(m, silu_ok).scalar_tensor_tensor(o2[t][:, s], ps[:, b, j * 128:(j + 1) * 128],
                                                                         st[:, 48 + 8 * t + k:49 + 8 * t + k], part2(t, 3)[:, s], ALU.mult, ALU.mult))
                bank_free[b] = [m2]
        aTh, aTl = over("aTh", W_at, 14336, [8, S]), over("aTl", W_at, 16384, [8, S])
        A.after(T.mark())
        transposes(8, lambda t, k: o2[t][:, k * 128:(k + 1) * 128], to_split(aTh, aTl), V.mark())

        T.after(ws_ok)
        for t in range(NT):
            for g in range(2):
                b = 6 + g
                T.after(*bank_free[b])
                for j in range(4):
                    k = 4 * g + j
                    m = T.eng.matmul(ps[:, b, j * 128:(j + 1) * 128], wsT[:, k * 128:(k + 1) * 128], part2(t, 5)[:, k * 128:(k + 1) * 128],
                                     start=True, stop=True)
                m = T.done(m)
                for j in range(4):
                    k = 4 * g + j
                    s = slice(k * 128, (k + 1) * 128)
                    bs = colv[:, COLS["b_spatial"] + k:COLS["b_spatial"] + k + 1]
                    m2 = V.done(V.after(m).scalar_tensor_tensor(part2(t, 4)[:, s], ps[:, b, j * 128:(j + 1) * 128], bs, part2(t, 4)[:, s], ALU.add, ALU.mult))
                bank_free[b] = [m2]
            V.done(V.after().tensor_tensor(part2(t, 4), part2(t, 4), part2(t, 6), ALU.mult))
        sTh = over("sTh", W_at, 0, [8, S])
        sTl = over("sTl", W_at, 7 * AW, [8, S])
        A.after(T.mark())
        transposes(8, lambda t, k: part2(t, 4)[:, k * 128:(k + 1) * 128], to_split(sTh, sTl), V.mark())
        T.after(V.mark(), A.mark())

        merged = B[:, :, 2048:4096]
        V.after(T.mark())

        def merge_body(i):
            cs = bass.ds(i * NC, NC)

            def gated(banks, got):
                before = V.mark()
                for t in range(NT):
                    A.done(A.after(got, before).activation(sg[:, t, :], banks[t], ACT.Sigmoid), evac if t else None)

            def first(banks, got):
                V.done(V.after(got, evac.mark()).tensor_tensor(merged[:, 0, cs], banks[0], sg[:, 0, :], ALU.mult))
                V.done(V.after().tensor_tensor(merged[:, 1, cs], banks[1], sg[:, 1, :], ALU.mult), evac)
                V.done(V.after().tensor_copy(st[:, 95:96], st[:, 0:1]))

            def second(banks, got):
                V.done(V.after(got, evac.mark()).tensor_tensor(sg[:, 0, :], banks[0], sg[:, 0, :], ALU.mult))
                V.done(V.after().tensor_tensor(sg[:, 1, :], banks[1], sg[:, 1, :], ALU.mult), evac)
                for t in range(NT):
                    V.done(V.after().tensor_tensor(merged[:, t, cs], merged[:, t, cs], sg[:, t, :], ALU.add))
            dense(4, gated)
            dense(2, first, lhs=(aTh, aTl))
            dense(4, gated)
            dense(2, second, lhs=(sTh, sTl))
        dense_loop(4, merge_body, 12, 4, {V.own: 5, A.own: 2})
        A.after(used.mark())
        transposes(DK, lambda t, k: merged[:, t, k * 128:(k + 1) * 128], to_split(xh, xl), V.mark(), evac.mark())
        T.after(V.mark())
        for n in range(4):
            def f(banks, got):
                for t in range(NT):
                    o = h[:, t, n * NC:(n + 1) * NC]
                    m = V.done(V.after(got).tensor_tensor(o, banks[t], o, ALU.add), evac if t else None)
                for t in range(NT):
                    A.after(m).dma_start(out[t * 128:(t + 1) * 128, n * NC:(n + 1) * NC], h[:, t, n * NC:(n + 1) * NC]).then_inc(loads["out"], 16)
            dense(4, f, last=(n == 3))
        assert used.count == CHUNKS == split_at[0]
        nc.scalar.wait_ge(loads["out"], 16 * 4 * NT)


def blocks_of(wt):
    K, N = wt.shape
    return wt.reshape(K // 512, 4, 128, N // NC, NC).transpose(3, 0, 2, 1, 4).reshape(-1, 128, CW)


def kernel(**inputs):
    import concourse.bacc as bacc
    from concourse.bass_utils import run_bass_kernel_spmd

    a = {k: np.asarray(v) for k, v in inputs.items()}
    f32 = np.float32
    a = {k: (v if k in ("x", "positions", "p") else v[0]) for k, v in a.items()}
    w_in, w_in_2 = a["w_in"], a["w_in_2"]
    rope = np.zeros((128, CW), f32)
    rope[:, :DK * QR] = w_in[:, D:].reshape(DK, 128, QR).transpose(1, 0, 2).reshape(128, DK * QR)
    pool = a["w_pool"].reshape(4, 2, 128, 256).transpose(2, 0, 1, 3).reshape(1, 128, CW)
    keys = np.stack([a["sub_k1"], a["sub_k2"]], 1).transpose(3, 0, 1, 2).reshape(1, 128, CW)
    proj = a["w_ple_proj"].reshape(2, 128, 4, NC).transpose(1, 2, 0, 3).reshape(128, 2, CW).transpose(1, 0, 2)
    n = AW
    ga, gb = blocks_of(w_in_2[:, 7 * n:7 * n + D]), blocks_of(w_in_2[:, 7 * n + D:])
    pa, pb = blocks_of(a["w_proj_a_2"]), blocks_of(a["w_proj_b_2"])
    merge = [c for i in range(4) for c in (ga[4 * i:4 * i + 4], pa[2 * i:2 * i + 2], gb[4 * i:4 * i + 4], pb[2 * i:2 * i + 2])]
    weights = np.concatenate([blocks_of(w_in[:, :D]), rope[None], pool, blocks_of(a["w_uq"]), blocks_of(a["w_ukv"]),
                              blocks_of(a["w_out"]), blocks_of(a["w_pq"]), keys, proj, blocks_of(a["w_ple_gate"]),
                              blocks_of(w_in_2[:, :7 * n])] + merge + [blocks_of(a["w_out_2"])])

    def col(v):
        return v.reshape(-1, 128).T
    cols = np.concatenate([col(a["mix_norm_gain"]), col(a["ple_norm_gain"]), col(a["norm_g_2"]), col(a["pool_scale"]),
                           col(a["q_lat_gain"]), col(a["kv_lat_gain"]), a["b_spatial_2"].T], 1)
    inv_freq = (f32(10000.0) ** (-np.arange(0, QR, 2, dtype=f32) / f32(QR))).astype(f32)
    rows = np.concatenate([a["q_norm_gain"], a["k_norm_gain"], a["q_norm_g_2"], a["k_norm_g_2"], a["sgu_norm_g_2"],
                           inv_freq, np.arange(16, dtype=f32)])[None]
    pool_op = np.zeros((S, 4, S), f32)
    for g, win in enumerate(POOL_WINDOWS):
        for t in range(S):
            lo = max(0, t - win + 1)
            pool_op[lo:t + 1, g, t] = f32(1) / f32(t + 1 - lo)
            pool_op[t, g, t] -= f32(1)
    arrays = dict(
        x=a["x"][0], cols=cols, rows=rows, positions=a["positions"].reshape(NT, 128).T, ffn_gain=a["ffn_norm_gain"][None],
        pool_op=pool_op.reshape(NT, 128, 4 * S).transpose(1, 0, 2).reshape(128, NT * 4 * S),
        p_t=a["p"][0, 0].T.reshape(2, 128, S).transpose(1, 0, 2).reshape(128, 2 * S),
        w_spatial_t=a["w_spatial_2"].transpose(2, 0, 1).reshape(128, 8 * 128),
        weights=weights, expert_u=a["expert_u"], expert_v=a["expert_v"])
    arrays = {k: np.ascontiguousarray(v) for k, v in arrays.items()}
    nc = bacc.Bacc("TRN2", target_bir_lowering=False, num_devices=1)
    aps = {k: nc.dram_tensor("in_" + k, v.shape, mybir.dt.from_np(v.dtype), kind="ExternalInput").ap() for k, v in arrays.items()}
    out = nc.dram_tensor("out", (S, D), F32, kind="ExternalOutput").ap()
    build(nc, out=out, **aps)
    r = run_bass_kernel_spmd(nc, [{"in_" + k: v for k, v in arrays.items()}], core_ids=[0])
    return r.results[0]["out"].reshape(1, S, D)
```

```python
from contextlib import ExitStack, contextmanager

import numpy as np
import concourse.bass as bass
from concourse import mybir

F32, F32R = mybir.dt.float32, mybir.dt.float32r
I32, U32 = mybir.dt.int32, mybir.dt.uint32
ALU, ACT = mybir.AluOpType, mybir.ActivationFunctionType
AX = mybir.AxisListType.X
ENG = mybir.EngineType

P128 = 128
S = 256
NT = S // P128
D = 2048
DK = D // P128
EPS = 1e-6
POOL_W, POOL_WINDOWS = 1024, (2, 4, 8, 16)
NH, QN, QR, LORA = 8, 128, 64, 512
QH = QN + QR
CHUNK = 64
TOPK, NKEYS, EXPERTS = 16, 128, 16384
PLE = 256
AW = 1024
CW = 2048
NC = 512
RAW = 4
SPL = 2
GR = 8
NEG = -1e30

N_CHUNKS = dict(w_in=16, w_rope=1, w_pool=1, w_uq=3, w_ukv=4, w_out=16, sub_k=1, w_pq=16, ple_proj=2, ple_gate=16,
                w_in_2=56, merge=48, w_out_2=16)
CHUNKS = sum(N_CHUNKS.values())

COLS, _at = {}, 0
for _n, _w in (("mix", 16), ("ffn", 16), ("ple", 16), ("norm2", 16), ("pool_scale", 8), ("q_lat", 4), ("kv_lat", 4),
               ("b_spatial", 8)):
    COLS[_n] = _at
    _at += _w
N_COLS = _at
ROWS, _at = {}, 0
for _n, _w in (("q_norm", QH), ("k_norm", QH), ("q_norm2", 128), ("k_norm2", 128), ("sgu", 128), ("inv_freq", 32),
               ("iota", 16)):
    ROWS[_n] = _at
    _at += _w
N_ROWS = _at


class Mark:
    def __init__(self, sem, const, per=0, i=None):
        self.sem, self.const, self.per, self.i = sem, const, per, i

    def value(self):
        return self.const if self.i is None or not self.per else self.i * self.per + self.const


class Counter:
    def __init__(self, sem, count=0):
        self.sem, self.count, self.start, self.per, self.i = sem, count, count, 0, None

    def mark(self, back=0):
        return Mark(self.sem, self.count - back, self.per, self.i)


class Lane:
    def __init__(self, eng, sem, chained=True):
        self.eng, self.own, self.chained, self.last = eng, Counter(sem), chained, []
        self.counters = [self.own]

    def after(self, *marks):
        for m in list(marks) + (self.last if self.chained else []):
            self.eng.wait_ge(m.sem, m.value())
        return self.eng

    def done(self, ins, counter=None):
        c = counter or self.own
        ins.then_inc(c.sem, 1)
        c.count += 1
        self.last = [c.mark()]
        return c.mark()

    def mark(self):
        return self.own.mark()


def build(nc, x, cols, rows, positions, ffn_gain, pool_op, p_t, w_spatial_t, weights, expert_u, expert_v, out):
    with ExitStack() as ctx:
        def sb(name, shape, dt=F32):
            return ctx.enter_context(nc.sbuf_tensor(name, shape, dt))

        def sem(name):
            return ctx.enter_context(nc.semaphore(name))

        def placed():
            return -(-nc.sbuf_base // 32) * 32

        def over(name, base, at, shape, dt=F32R):
            return nc.alloc_sbuf_tensor_at(name, [128] + shape, dt, offset=base + 4 * at)

        raw = sb("raw", [128, RAW, CW])
        whi = sb("whi", [128, SPL, CW], F32R)
        wlo = sb("wlo", [128, SPL, CW], F32R)
        xT_at = placed()
        xT = sb("xT", [128, 2, DK * S], F32R)
        h = sb("h", [128, NT, D])
        W_at = placed()
        W = sb("W", [128, 20736])
        colv = sb("colv", [128, N_COLS])
        rowv = sb("rowv", [128, N_ROWS])
        ident = sb("ident", [128, 128])
        mask = sb("mask", [128, 2, 256])
        tmp = sb("tmp", [128, 1024])
        pos = sb("pos", [128, NT], I32)
        trig = sb("trig", [128, 2, NT, 32])
        st = sb("st", [128, 96])
        idx = sb("idx", [128, NT, 128], I32)
        gate = sb("gate", [128, NT, 128])
        act = sb("act", [128, NT, 128])
        idx_now = sb("idx_now", [128, 16], I32)
        col_now = sb("col_now", [128, 16])
        ps = ctx.enter_context(nc.psum_tensor("ps", [128, 8, 512], F32))

        xh = xT[:, 0, :].rearrange("p (k s) -> p k s", k=DK)
        xl = xT[:, 1, :].rearrange("p (k s) -> p k s", k=DK)

        def w(at, *shape):
            n = int(np.prod(shape))
            v = W[:, at:at + n]
            if len(shape) == 2:
                v = v.rearrange("p (a b) -> p a b", a=shape[0])
            elif len(shape) == 3:
                v = v.rearrange("p (a b c) -> p a b c", a=shape[0], b=shape[1])
            return v

        def row(name, n):
            return rowv[:, ROWS[name]:ROWS[name] + n]

        V = Lane(nc.vector, sem("v_done"))
        A = Lane(nc.scalar, sem("a_done"))
        T = Lane(nc.tensor, sem("t_done"), chained=False)
        G = Lane(nc.gpsimd, sem("p_done"))
        hi_done = Counter(sem("hi_done"))
        lo_done = Counter(sem("lo_done"))
        used = Counter(sem("used"))
        evac = Counter(sem("evac"))
        rows_used = Counter(sem("rows_used"), GR)
        A.counters += [hi_done, evac]
        V.counters += [lo_done, evac, rows_used]
        T.counters += [used]
        landed = [sem(f"landed{r}") for r in range(RAW)]
        row_in = [sem(f"row_in{r}") for r in range(GR)]
        loads = {n: sem("load_" + n) for n in ("x", "cols", "rows", "pos", "pool_op", "p", "ffn", "ws", "out")}
        everything = [V.own, A.own, T.own, G.own, hi_done, lo_done, used, evac, rows_used]

        @contextmanager
        def loop(n, per, lanes):
            base = {c: c.count for c in everything}
            with nc.Fori(0, n, engines=[{V: ENG.DVE, A: ENG.Activation, T: ENG.PE, G: ENG.Pool}[k] for k in lanes]) as i:
                for c, k in per.items():
                    c.per, c.i = k, i
                for k in lanes:
                    k.last = [c.mark() for c in k.counters if c.count != c.start or c in per]
                yield i
                got = {c: c.count - base[c] for c in everything if c.count != base[c]}
                assert got == per, sorted((c.sem.name, v) for c, v in got.items())
            for c, k in per.items():
                c.per, c.i, c.count = 0, None, base[c] + k * n
            for k in lanes:
                k.last = [c.mark() for c in k.counters if c.count != c.start or c in per]

        def load(name, dst, src, *marks):
            for m in marks:
                nc.scalar.wait_ge(m.sem, m.value())
            nc.scalar.dma_start(dst, src).then_inc(loads[name], 16)
            return Mark(loads[name], 16)

        for t in range(NT):
            nc.sync.dma_start(h[:, t, :], x[t * 128:(t + 1) * 128, :]).then_inc(loads["x"], 16)
        x_in = Mark(loads["x"], 16 * NT)
        for c in range(RAW):
            nc.sync.dma_start(raw[:, c, :], weights[c]).then_inc(landed[c], 16)
        assert CHUNKS % RAW == 0
        with nc.Fori(0, CHUNKS // RAW - 1, engines=[ENG.SP]) as g:
            for r in range(RAW):
                nc.sync.wait_ge(used.sem, g * RAW + (r + 1))
                nc.sync.dma_start(raw[:, r, :], weights[bass.ds(g * RAW + (RAW + r), 1)].rearrange("a p n -> p (a n)"))\
                    .then_inc(landed[r], 16)

        cols_in = load("cols", colv[:, :], cols)
        rows_in = load("rows", rowv[:, :], rows.broadcast_to([128, N_ROWS]))
        pos_in = load("pos", pos[:, :], positions)
        POOL_OP = w(15488, 2, 4, 256)
        pool_in = load("pool_op", W[:, 15488:15488 + 2048], pool_op)

        G.done(G.after().memset(tmp[:, 0:128], 1.0))
        ident_ok = G.done(G.after().affine_select(out=ident[:, :], in_=tmp[:, 0:128], compare_op=ALU.is_equal, fill=0.0,
                                                  base=0, pattern=[[-1, 128]], channel_multiplier=1))
        G.done(G.after().memset(mask[:, :, :], 0.0))
        G.done(G.after().memset(mask[0:CHUNK, 0, 128 + CHUNK:256], NEG))
        mask_ok = G.done(G.after().affine_select(out=mask[:, 1, 128:256], in_=mask[:, 1, 128:256], compare_op=ALU.is_ge,
                                                 fill=NEG, base=0, pattern=[[-1, 128]], channel_multiplier=1))
        T.after(ident_ok)
        V.after(cols_in, rows_in)
        A.after(cols_in)

        split_at = [0]

        def split_next(A=A, V=V):
            c = split_at[0]
            r, b = c % RAW, c % SPL
            per = hi_done.per
            here = Mark(landed[r], 16 * (c // RAW + 1), 16 * per // RAW if per else 0, hi_done.i)
            free = [Mark(used.sem, c - SPL + 1, per, hi_done.i)] if c >= SPL else []
            hi = A.done(A.after(here, *free).activation(whi[:, b, :], raw[:, r, :], ACT.Copy), hi_done)
            V.done(V.after(hi).tensor_tensor(wlo[:, b, :], raw[:, r, :], whi[:, b, :].bitcast(F32), ALU.subtract), lo_done)
            split_at[0] += 1

        def next_chunk(last=False):
            c = used.count
            if not last:
                split_next()
            T.after(Mark(lo_done.sem, c + 1, used.per, used.i))
            return whi[:, c % SPL, :], wlo[:, c % SPL, :]

        def enter(n_chunks):
            pass

        def products(out_ap, a, b, start, stop):
            T.eng.matmul(out_ap, a[0], b[0], start=start, stop=False)
            T.eng.matmul(out_ap, a[0], b[1], start=False, stop=False)
            return T.eng.matmul(out_ap, a[1], b[0], start=False, stop=stop)

        pairs = [0]

        def dense_steps(n_q, evacuate, q0=0, cols_n=NC, lhs=None, last=False):
            lh, ll = lhs or (xh, xl)
            pair = 2 * (pairs[0] % 2)
            if pairs[0] >= 2:
                T.after(Mark(evac.sem, pairs[0] - 1, evac.per, evac.i))
            pairs[0] += 1
            for q in range(n_q):
                hi, lo = next_chunk(last=last and q == n_q - 1)
                nk = min(CW // cols_n, 4 if cols_n == NC else DK)
                for k in range(nk):
                    for t in range(NT):
                        o = ps[:, pair + t, 0:cols_n]
                        s = slice(t * 128, (t + 1) * 128)
                        cs = slice(k * cols_n, (k + 1) * cols_n)
                        ks = q0 + q * 4 + k
                        m = products(o, (lh[:, ks, s], ll[:, ks, s]), (hi[:, cs], lo[:, cs]),
                                     start=(q == 0 and k == 0), stop=(q == n_q - 1 and k == nk - 1))
                got = T.done(m, used)
                if q < n_q - 1:
                    yield
            evacuate([ps[:, pair + t, 0:cols_n] for t in range(NT)], got)
            yield

        def dense(*args, **kw):
            for _ in dense_steps(*args, **kw):
                pass

        side = [iter(())]

        def tick(n=1):
            for _ in range(n):
                next(side[0], None)

        def side_done():
            for _ in side[0]:
                pass

        def dense_loop(n, body, chunks, blocks, per):
            assert chunks % RAW == 0 and blocks % 2 == 0
            c0, p0 = split_at[0], pairs[0]
            full = {hi_done: chunks, lo_done: chunks, used: chunks, evac: blocks}
            full.update(per)
            with loop(n, full, [V, A, T]) as i:
                body(i)
            split_at[0], pairs[0] = c0 + n * chunks, p0 + n * blocks

        def copy_out(dst, scale=None):
            def f(banks, got):
                for t in range(NT):
                    e = V.after(got)
                    if scale is None:
                        ins = e.tensor_copy(dst(t), banks[t])
                    else:
                        ins = e.tensor_scalar(dst(t), banks[t], st[:, scale + t:scale + t + 1], None, ALU.mult)
                    V.done(ins, evac if t else None)
            return f

        bank_free = {b: [] for b in range(8)}

        def transposes(n, src, put, *marks, wide=None):
            T.after(*marks)
            for g in range(n // 2):
                b = 4 + g % 4
                T.after(*bank_free[b])
                for k in range(2):
                    for t in range(NT):
                        m = T.eng.transpose(ps[:, b, (2 * k + t) * 128:(2 * k + t + 1) * 128], src(t, 2 * g + k), ident[:, :])
                bank_free[b] = put(g, ps[:, b, :], T.done(m))

        def two(ap, g):
            return ap[:, 2 * g:2 * g + 2, :].rearrange("p k s -> p (k s)")

        def to_split(hi, lo, gain=None):
            def put(g, bank, got):
                if gain is None:
                    m = A.done(A.after(got).activation(two(hi, g), bank, ACT.Copy))
                    m = V.done(V.after(m).tensor_tensor(two(lo, g), bank, two(hi, g).bitcast(F32), ALU.subtract))
                else:
                    s = [colv[:, gain + 2 * g + k:gain + 2 * g + k + 1] for k in range(2)]
                    for k in range(2):
                        m = A.done(A.after(got).activation(hi[:, 2 * g + k, :], bank[:, k * S:(k + 1) * S], ACT.Copy, scale=s[k]))
                    for k in range(2):
                        m = V.done(V.after(m).scalar_tensor_tensor(lo[:, 2 * g + k, :], bank[:, k * S:(k + 1) * S], s[k],
                                                                   hi[:, 2 * g + k, :].bitcast(F32), ALU.mult, ALU.subtract))
                return [m]
            return put

        def to_plain(dst):
            def put(g, bank, got):
                if g % 2:
                    return [A.done(A.after(got).activation(dst[:, g * 512:(g + 1) * 512], bank, ACT.Copy))]
                return [V.done(V.after(got).tensor_copy(dst[:, g * 512:(g + 1) * 512], bank))]
            return put

        def rstd(ss, n, *marks):
            m = V.done(V.after(*marks).tensor_scalar(ss, ss, 1.0 / n, EPS, ALU.mult, ALU.add))
            m = A.done(A.after(m).activation(ss, ss, ACT.Sqrt))
            return V.done(V.after(m).reciprocal(ss, ss))

        RSTD = 0

        def row_rstd():
            for t in range(NT):
                m = A.done(A.after(V.mark(), T.mark(), *[m for b in range(4, 8) for m in bank_free[b]])
                           .activation(ps[:, 4:8, :].rearrange("p a b -> p (a b)"), h[:, t, :], ACT.Square, accum_out=st[:, RSTD + t:RSTD + t + 1]))
            for b in range(4, 8):
                bank_free[b] = [m]
            return rstd(st[:, RSTD:RSTD + NT], D, m)

        def enter_block(gain, *marks):
            A.after(used.mark())
            transposes(DK, lambda t, k: h[:, t, k * 128:(k + 1) * 128], to_split(xh, xl, gain), *marks)
            xT_ok = V.mark()
            row_rstd()
            T.after(xT_ok)

        enter_block(COLS["mix"], x_in)
        split_next()
        Z_W = D + QR
        z = w(0, NT, Z_W)

        def z_body(i):
            for j in range(2):
                dense(4, copy_out(lambda t: z[:, t, bass.ds(i * (2 * NC) + j * NC, NC)], RSTD))
        V.after(T.mark())
        dense_loop(2, z_body, 8, 2, {V.own: 2})
        dense(1, copy_out(lambda t: z[:, t, D:Z_W], RSTD), cols_n=QR)
        z_ok = evac.mark()

        A.after(used.mark())
        transposes(8, lambda t, k: z[:, t, POOL_W + k * 128:POOL_W + (k + 1) * 128],
                   to_split(xh[:, 8:16, :], xl[:, 8:16, :], COLS["q_lat"]), z_ok)
        lat_ok = V.mark()
        for j in range(2):
            for t in range(NT):
                c = POOL_W + j * LORA
                m = A.done(A.after(z_ok).activation(tmp[:, 0:LORA], z[:, t, c:c + LORA], ACT.Square, accum_out=st[:, 4 + 2 * j + t:5 + 2 * j + t]))
        rstd(st[:, 4:8], LORA, m)

        dTh, dTl = over("dTh", W_at, 11392, [8, S]), over("dTl", W_at, 13440, [8, S])
        T.after(z_ok, pool_in)
        for k in range(8):
            b = 6 + k % 2
            T.after(*bank_free[b])
            for t in range(NT):
                m = T.eng.matmul(ps[:, b, 0:S], z[:, t, k * 128:(k + 1) * 128], POOL_OP[:, t, k // 2, :], start=(t == 0), stop=(t == 1))
            m = A.done(A.after(T.done(m)).activation(dTh[:, k, :], ps[:, b, 0:S], ACT.Copy))
            bank_free[b] = [V.done(V.after(m).tensor_tensor(dTl[:, k, :], ps[:, b, 0:S], dTh[:, k, :].bitcast(F32), ALU.subtract))]

        phi, plo = next_chunk()
        for k in range(8):
            b = 6 + k % 2
            g, half = k // 2, k % 2
            T.after(*bank_free[b], *([V.mark()] if k == 0 else []))
            for c in range(2):
                col = (g * 2 + c) * 256 + half * 128
                m = products(ps[:, b, 0:S], (phi[:, col:col + 128], plo[:, col:col + 128]), (dTh[:, 2 * g + c, :], dTl[:, 2 * g + c, :]),
                             start=(c == 0), stop=(c == 1))
            m = T.done(m, used if k == 7 else None)
            s = colv[:, COLS["pool_scale"] + k:COLS["pool_scale"] + k + 1]
            m = A.done(A.after(m).activation(xh[:, k, :], ps[:, b, 0:S], ACT.Copy, scale=s))
            bank_free[b] = [V.done(V.after(m).scalar_tensor_tensor(xl[:, k, :], ps[:, b, 0:S], s, xh[:, k, :].bitcast(F32), ALU.mult, ALU.subtract))]

        q = w(4224, NT, NH * QH)
        kv = w(7296, NT, NH * 256)
        T.after(lat_ok)
        for n in range(3):
            dense(1, copy_out(lambda t: q[:, t, n * NC:(n + 1) * NC], 4), q0=8)
        q_ok = evac.mark()
        for n in range(4):
            dense(1, copy_out(lambda t: kv[:, t, n * NC:(n + 1) * NC], 6), q0=12)

        kv_ok = evac.mark()

        def residual_in(at):
            def f(banks, got):
                for t in range(NT):
                    V.done(V.after(got).tensor_tensor(h[:, t, at], banks[t], h[:, t, at], ALU.add), evac if t else None)
            return f

        def pool_half():
            for n in range(4):
                yield from dense_steps(2, residual_in(slice(n * NC, (n + 1) * NC)))
        T.after(V.mark())
        side[0] = pool_half()

        TWO_PI = 2 * np.pi
        C1 = 6.28125
        C2 = float(np.float32(np.round((TWO_PI - C1) * 2 ** 19) / 2 ** 19))
        C3 = float(TWO_PI - C1 - C2)
        ang, turns = tmp[:, 0:64].rearrange("p (t f) -> p t f", t=NT), tmp[:, 64:128].rearrange("p (t f) -> p t f", t=NT)
        V.done(V.after(pos_in, A.mark()).tensor_copy(st[:, 8:8 + NT], pos[:, :]))
        for t in range(NT):
            V.done(V.after().tensor_scalar(ang[:, t, :], row("inv_freq", 32), st[:, 8 + t:9 + t], None, ALU.mult))
        V.done(V.after().tensor_scalar(turns, ang, 1.0 / TWO_PI, 12582912.0, ALU.mult, ALU.add))
        V.done(V.after().tensor_scalar(turns, turns, 12582912.0, None, ALU.subtract))
        for c in (C1, C2, C3):
            V.done(V.after().scalar_tensor_tensor(ang, turns, -c, ang, ALU.mult, ALU.add))
        V.done(V.after().tensor_scalar(trig[:, 1, :, :], ang, 3.1415925, -3.1415925, ALU.min, ALU.max))
        V.done(V.after().tensor_scalar(ang, ang, float(np.pi / 2), None, ALU.add))
        V.done(V.after().tensor_scalar(turns, ang, float(np.pi), -TWO_PI, ALU.is_gt, ALU.mult))
        V.done(V.after().tensor_tensor(ang, ang, turns, ALU.add))
        m = V.done(V.after().tensor_scalar(trig[:, 0, :, :], ang, 3.1415925, -3.1415925, ALU.min, ALU.max))
        trig_ok = A.done(A.after(m).activation(trig[:, :, :, :], trig[:, :, :, :], ACT.Sin))

        def heads(ap, n):
            return ap.rearrange("p (h d) -> p h d", h=n)

        def per_head(ap, n, d):
            return ap.unsqueeze(2).broadcast_to([128, n, d])

        def per_dim(ap, n, d):
            return ap.unsqueeze(1).broadcast_to([128, n, d])

        junk = ps[:, 4:8, :].rearrange("p a b -> p (a b)")

        def junk_free():
            return [m for b in range(4, 8) for m in bank_free[b]]

        def set_junk(m):
            for b in range(4, 8):
                bank_free[b] = [m]

        qrh = w(18560, NT, NH * QR)
        krh = w(19584, NT, NH * QR)
        rot_a = tmp[:, 256:512]
        rot_b = tmp[:, 512:768]

        def rotate(dst, src, t, n):
            half = QR // 2
            cos, sin = per_dim(trig[:, 0, t, :], n, half), per_dim(trig[:, 1, t, :], n, half)
            a, b = heads(rot_a[:, 0:n * half], n), heads(rot_b[:, 0:n * half], n)
            x1, x2 = src[:, :, 0:half], src[:, :, half:QR]
            for o, (u, v_), op in ((dst[:, :, 0:half], (x1, x2), ALU.subtract), (dst[:, :, half:QR], (x2, x1), ALU.add)):
                V.done(V.after(trig_ok).tensor_tensor(a, u, cos, ALU.mult))
                V.done(V.after().tensor_tensor(b, v_, sin, ALU.mult))
                m = V.done(V.after().tensor_tensor(o, a, b, op))
            return m

        for t in range(NT):
            qt = heads(q[:, t, :], NH)
            m = A.done(A.after(q_ok, *junk_free()).activation(junk[:, 0:NH * QH], q[:, t, :], ACT.Square))
            ss = st[:, 16:24]
            m = V.done(V.after(m).tensor_reduce(ss, heads(junk[:, 0:NH * QH], NH), AX, ALU.add))
            set_junk(m)
            rstd(ss, QH)
            V.done(V.after().tensor_tensor(qt, qt, per_head(ss, NH, QH), ALU.mult))
            V.done(V.after().tensor_tensor(qt, qt, per_dim(row("q_norm", QH), NH, QH), ALU.mult))
            rotate(heads(qrh[:, t, :], NH), qt[:, :, QN:QH], t, NH)
            tick()
            kt = heads(kv[:, t, :], NH)
            kr = z[:, t, D:Z_W]
            m = A.done(A.after(kv_ok, *junk_free()).activation(junk, kv[:, t, :], ACT.Square))
            m2 = A.done(A.after(V.mark()).activation(tmp[:, 768:768 + QR], kr, ACT.Square, accum_out=st[:, 32:33]))
            ss = st[:, 24:32]
            m = V.done(V.after(m, m2).tensor_reduce(ss, heads(junk, NH)[:, :, 0:QN], AX, ALU.add))
            set_junk(m)
            V.done(V.after().tensor_scalar(ss, ss, st[:, 32:33], None, ALU.add))
            rstd(ss, QH)
            V.done(V.after().tensor_tensor(kt[:, :, 0:QN], kt[:, :, 0:QN], per_head(ss, NH, QN), ALU.mult))
            V.done(V.after().tensor_tensor(kt[:, :, 0:QN], kt[:, :, 0:QN], per_dim(row("k_norm", QH)[:, 0:QN], NH, QN), ALU.mult))
            kg, kr2 = tmp[:, 128:192], tmp[:, 192:256]
            V.done(V.after().tensor_tensor(kg, kr, row("k_norm", QH)[:, QN:QH], ALU.mult))
            rotate(kr2.unsqueeze(1), kg.unsqueeze(1), t, 1)
            V.done(V.after().tensor_tensor(heads(krh[:, t, :], NH), per_dim(kr2, NH, QR), per_head(ss, NH, QR), ALU.mult))
            tick()

        qT, qrT = W[:, 11392:13440], W[:, 13440:14464]
        kT, krT = W[:, 0:2048], W[:, 2048:3072]
        A.after(T.mark(), used.mark())
        V.after(T.mark(), used.mark())
        ok = V.mark()
        transposes(NH, lambda t, k: q[:, t, k * QH:k * QH + QN], to_plain(qT), ok)
        transposes(NH, lambda t, k: kv[:, t, k * 256:k * 256 + QN], to_plain(kT), ok)
        transposes(NH // 2, lambda t, k: qrh[:, t, k * 128:(k + 1) * 128], to_plain(qrT), ok)
        transposes(NH // 2, lambda t, k: krh[:, t, k * 128:(k + 1) * 128], to_plain(krT), ok)

        def softmax(n_heads, n_keys, scale, t, score, which, p_out, sums, normed, ticks=0):
            per = 2
            for g in range(n_heads // per):
                b = 6 + g % 2
                T.after(*bank_free[b])
                k = 4 * (g // 2) + g % 2
                for j in range(per):
                    m = score(k + 2 * j, ps[:, b, j * n_keys:(j + 1) * n_keys])
                src = ps[:, b, 0:per * n_keys].rearrange("p (a k) -> p a k", a=per)
                dst = p_out[:, k:k + 3:2, :]
                msk = per_dim(mask[:, which, 256 - n_keys:256], per, n_keys)
                m = V.done(V.after(T.done(m), mask_ok).tensor_tensor(dst, src, msk, ALU.add))
                bank_free[b] = [m]
                if g % 2:
                    tick()
            mx = st[:, 40:48]
            V.done(V.after().tensor_reduce(mx, p_out, AX, ALU.max))
            nm = V.done(V.after(A.mark()).tensor_scalar(mx, mx, -scale, None, ALU.mult))
            for k in range(n_heads):
                m = A.done(A.after(nm).activation(p_out[:, k, :], p_out[:, k, :], ACT.Exp, bias=mx[:, k:k + 1], scale=scale,
                                                  accum_out=sums[:, k:k + 1]))
            m = V.done(V.after(m).reciprocal(sums, sums))
            tick(ticks)
            if normed:
                m = V.done(V.after().tensor_tensor(p_out, p_out, per_head(sums, n_heads, n_keys), ALU.mult))
            return m

        def turn_probabilities(p_of, dst_of, ok):
            for k in range(NH):
                b = 4 + k % 4
                T.after(ok, *bank_free[b])
                for j, (t, kt_) in enumerate(((0, 0), (1, 0), (1, 1))):
                    m = T.eng.transpose(ps[:, b, j * 128:(j + 1) * 128], p_of(t)[:, k, kt_ * 128:(kt_ + 1) * 128], ident[:, :])
                m = T.done(m)
                if k % 4 == 3:
                    tick()
                if k % 2:
                    bank_free[b] = [V.done(V.after(m).tensor_copy(dst_of(k), ps[:, b, 0:384]))]
                else:
                    bank_free[b] = [A.done(A.after(m).activation(dst_of(k), ps[:, b, 0:384], ACT.Copy))]

        prob = [w(15488, NH, 128), w(16512, NH, 256)]
        pT = w(4224, NH, 384)
        T.after(A.mark(), V.mark())

        def mla_score(t):
            def f(k, o):
                keys, qs = (t + 1) * 128, slice(t * 128, (t + 1) * 128)
                T.eng.matmul(o, qT[:, k * S:(k + 1) * S][:, qs], kT[:, k * S:k * S + keys], start=True, stop=False)
                r = slice(64 * (k % 2), 64 * (k % 2) + 64)
                at = (k // 2) * S
                return T.eng.matmul(o, qrT[r, at:at + S][:, qs], krT[r, at:at + keys], start=False, stop=True)
            return f

        for t in range(NT):
            ok = softmax(NH, (t + 1) * 128, QH ** -0.5, t, mla_score(t), 0, prob[t], st[:, 48:56], True)
        V.after(T.mark())
        A.after(T.mark())
        turn_probabilities(lambda t: prob[t], lambda k: pT[:, k, :], ok)
        T.after(A.mark(), V.mark())
        for g in range(NH // 2):
            b = 6 + g % 2
            T.after(*bank_free[b])
            for j in range(2):
                k = 2 * g + j
                v_of = [kv[:, kt_, k * 256 + QN:(k + 1) * 256] for kt_ in range(2)]
                T.eng.matmul(ps[:, b, j * S:j * S + 128], v_of[0], pT[:, k, 0:128], start=True, stop=True)
                for kt_ in range(2):
                    m = T.eng.matmul(ps[:, b, j * S + 128:(j + 1) * S], v_of[kt_], pT[:, k, 128 + kt_ * 128:256 + kt_ * 128],
                                     start=(kt_ == 0), stop=(kt_ == 1))
            bank_free[b] = to_split(xh[:, 8:16, :], xl[:, 8:16, :])(g, ps[:, b, :], T.done(m))
        T.after(V.mark())

        side_done()

        def residual_body(i):
            for j in range(2):
                dense(2, residual_in(bass.ds(i * (2 * NC) + j * NC, NC)), q0=8)
        dense_loop(2, residual_body, 4, 2, {V.own: 2})

        xn = w(0, NT, D)
        ffn_row = W[:, 14336:14336 + D]
        ffn_in = load("ffn", ffn_row, ffn_gain.broadcast_to([128, D]), V.mark(), T.mark(), A.mark(), evac.mark())
        KH, KL = over("KH", W_at, 16384, [CW]), over("KL", W_at, 18432, [CW])
        khi, klo = next_chunk()
        A.after(T.mark(), V.mark())
        m = A.done(A.after(Mark(lo_done.sem, used.count + 1)).activation(KH[:, :], khi, ACT.Copy))
        m = V.done(V.after(m).tensor_copy(KL[:, :], klo))
        T.after(m)
        T.done(T.eng.transpose(ps[:, 4, 0:128], ident[:, :], ident[:, :]), used)
        enter_block(COLS["ffn"], evac.mark(), *[m for m in bank_free[4]])

        qb = [w(4096 + k * 1024, NT, NC) for k in range(2)]
        qh, ql = over("qh", W_at, 6144, [4, S]), over("ql", W_at, 7168, [4, S])
        s0 = W[:, 8192:8192 + NC]
        s1 = W[:, 12288:12288 + D]

        def queries():
            for n in range(4):
                yield from dense_steps(4, copy_out(lambda t: qb[n % 2][:, t, :], RSTD))
        side[0] = queries()
        tick()
        for t in range(NT):
            V.done(V.after(ffn_in).scalar_tensor_tensor(xn[:, t, :], h[:, t, :], st[:, RSTD + t:RSTD + t + 1], ffn_row, ALU.mult, ALU.mult))
        tick(3)

        def piece(at, *shape):
            v = tmp[:, at:at + int(np.prod(shape))]
            return v.rearrange("p (a b) -> p a b", a=shape[0]) if len(shape) == 2 else v
        s_now = piece(0, 2, NKEYS)
        cand, hot = piece(256, 256), piece(512, 16, 16)
        best, best_u, best_f = piece(768, 2, 16), piece(800, 2, 16).bitcast(U32), piece(832, 2, 16)
        top, top_u = piece(864, 16), piece(880, 16).bitcast(U32)
        part_u = [piece(896, 16).bitcast(U32), piece(912, 16).bitcast(U32)]
        part_f, e_f = [piece(928, 16), piece(944, 16)], [piece(960, 16), piece(976, 16)]

        def top16(vals, out_v, out_i):
            def after():
                V.after()
                if V.own.i is not None:
                    V.eng.nop(nofuse=True)
                return V.eng
            V.done(after().max(out_v[:, 0:8], vals))
            V.done(after().max_index(out_i[:, 0:8], out_v[:, 0:8], vals))
            V.done(after().match_replace(vals, out_v[:, 0:8], vals, -3.0e38))
            V.done(after().max(out_v[:, 8:16], vals))
            return V.done(after().max_index(out_i[:, 8:16], out_v[:, 8:16], vals))

        def best_keys(scores, *marks):
            V.after(*marks)
            for j in range(2):
                top16(scores[:, j, :], best[:, j, :], best_u[:, j, :])
            return V.done(V.after().tensor_copy(best_f, best_u))

        def best_experts(idx_out):
            V.done(V.after().tensor_tensor(cand.rearrange("p (a b) -> p a b", a=16), best[:, 0, :].unsqueeze(2).broadcast_to([128, 16, 16]),
                                           best[:, 1, :].unsqueeze(1).broadcast_to([128, 16, 16]), ALU.add))
            top16(cand, top, top_u)
            V.done(V.after().tensor_scalar(part_u[0], top_u, 4, None, ALU.logical_shift_right))
            V.done(V.after().tensor_scalar(part_u[1], top_u, 15, None, ALU.bitwise_and))
            for j in range(2):
                V.done(V.after().tensor_copy(part_f[j], part_u[j]))
                V.done(V.after().tensor_tensor(hot, part_f[j].unsqueeze(2).broadcast_to([128, 16, 16]),
                                               row("iota", 16).unsqueeze(1).broadcast_to([128, 16, 16]), ALU.is_equal))
                V.done(V.after().tensor_tensor(hot, hot, best_f[:, j, :].unsqueeze(1).broadcast_to([128, 16, 16]), ALU.mult))
                V.done(V.after().tensor_reduce(e_f[j], hot, AX, ALU.add))
            V.done(V.after().scalar_tensor_tensor(e_f[0], e_f[0], float(NKEYS), e_f[1], ALU.mult, ALU.add))
            return V.done(V.after().tensor_copy(idx_out, e_f[0]))

        for n in range(4):
            A.after(T.mark())
            transposes(4, lambda t, k: qb[n % 2][:, t, k * 128:(k + 1) * 128], to_split(qh, ql), evac.mark())
            T.after(V.mark())
            tick()
            for t in range(NT):
                T.after(*bank_free[6 + t])
                for k in range(4):
                    s = slice(t * 128, (t + 1) * 128)
                    c = slice((4 * n + k) * 128, (4 * n + k + 1) * 128)
                    m = products(ps[:, 6 + t, k * 128:(k + 1) * 128], (qh[:, k, s], ql[:, k, s]), (KH[:, c], KL[:, c]), start=True, stop=True)
                m = T.done(m)
                dst = s0 if t == 0 else s1[:, n * NC:(n + 1) * NC]
                bank_free[6 + t] = [A.done(A.after(m, V.mark()).activation(dst, ps[:, 6 + t, :], ACT.Copy))]
                if t == 0:
                    s0_ok = bank_free[6][0]
            tick()
            for k in range(2):
                hd = 2 * n + k
                best_keys(s0[:, k * 256:(k + 1) * 256].rearrange("p (a b) -> p a b", a=2), s0_ok)
                best_experts(idx[:, 0, hd * 16:(hd + 1) * 16])
                V.done(V.after().tensor_copy(gate[:, 0, hd * 16:(hd + 1) * 16], top))
                tick()
        side_done()
        idx_ok = [V.mark(), None]
        pq_done = [used.mark(), A.mark(), T.mark()]

        proj = w(16384, NT, D)
        pTs = w(14848, 2, S)
        pTh, pTl = over("pTh", W_at, 15360, [2, S]), over("pTl", W_at, 15872, [2, S])
        p_in = load("p", pTs, p_t.rearrange("p (k s) -> p k s", k=2), V.mark())
        m = A.done(A.after(p_in).activation(pTh[:, :, :], pTs, ACT.Copy))
        m = V.done(V.after(m).tensor_tensor(pTl[:, :, :], pTs, pTh[:, :, :].bitcast(F32), ALU.subtract))
        T.after(m)
        keys_read = T.mark()
        for c in range(2):
            hi, lo = next_chunk()
            for n in range(2):
                pair = 2 * (pairs[0] % 2)
                T.after(Mark(evac.sem, pairs[0] - 1))
                for t in range(NT):
                    for k in range(2):
                        cs = slice((n * 2 + k) * NC, (n * 2 + k + 1) * NC)
                        m = products(ps[:, pair + t, :], (pTh[:, k, t * 128:(t + 1) * 128], pTl[:, k, t * 128:(t + 1) * 128]),
                                     (hi[:, cs], lo[:, cs]), start=(k == 0), stop=(k == 1))
                m = T.done(m, used if n == 1 else None)
                pairs[0] += 1
                for t in range(NT):
                    A.done(A.after(m, keys_read).activation(proj[:, t, (2 * c + n) * NC:(2 * c + n + 1) * NC], ps[:, pair + t, :], ACT.Copy),
                           evac if t else None)

        xT_rows = over("xT_rows", xT_at, 0, [4, D], F32)
        slots = [W[:, 4096 + r * D:4096 + (r + 1) * D] for r in range(4)] + [xT_rows[:, r, :] for r in range(4)]
        best1, best1_f = W[:, 14336:14592], W[:, 14592:14848]
        G.after(*pq_done)
        G.eng.sem_inc(rows_used.sem, GR)
        V.after(bank_free[6][0], bank_free[7][0])

        def peer_pass(t, table, use, beside, v_per, a_per):
            G.after(idx_ok[t])
            lanes = [G, V] + ([A] if a_per else [])
            per = {G.own: 4, V.own: v_per, rows_used: 16}
            if a_per:
                per[A.own] = a_per
            with loop(NH, per, lanes) as i:
                first = rows_used.count - GR
                use(i, None, None, None)
                for j in range(16):
                    r = j % GR
                    free = Mark(rows_used.sem, first + j + 1, 16, i)
                    if j % 4 == 0:
                        ready = G.done(G.after(free).tensor_copy(idx_now[:, j:j + 4], idx[:, t, bass.ds(i * 16 + j, 4)]))
                    for m in (free, ready):
                        G.eng.wait_ge(m.sem, m.value())
                    G.eng.nop(nofuse=True)
                    G.eng.indirect_dma_start(slots[r], None, table[:, :],
                                             bass.IndirectOffsetOnAxis(idx_now[:, j:j + 1], 0)).then_inc(row_in[r], 16)
                    use(i, j, slots[r], Mark(row_in[r], 16 * ((first + j) // GR + 1), 32, i))
                    if beside:
                        beside(i, j)

        def dot(t):
            def f(i, j, r, m):
                if j is None:
                    return
                V.done(V.after(m).tensor_tensor_reduce(junk, r, xn[:, t, :], 1.0, 0.0, ALU.mult, ALU.add, col_now[:, j:j + 1]), rows_used)
                if j == 15:
                    V.done(V.after().tensor_copy(act[:, t, bass.ds(i * 16, 16)], col_now[:, :]))
            return f

        def add_row(t):
            def f(i, j, r, m):
                if j is None:
                    V.done(V.after().tensor_copy(col_now[:, :], act[:, t, bass.ds(i * 16, 16)]))
                    return
                V.done(V.after(m).scalar_tensor_tensor(h[:, t, :], r, col_now[:, j:j + 1], h[:, t, :], ALU.mult, ALU.add), rows_used)
            return f

        def select_keys(i, j):
            if j == 2:
                s_ok = A.done(A.after(V.mark()).activation(tmp[:, 0:256], s1[:, bass.ds(i * 256, 256)], ACT.Copy))
                m = best_keys(s_now, s_ok)
                A.done(A.after(m).activation(best1[:, bass.ds(i * 32, 32)], tmp[:, 768:800], ACT.Copy))
                A.done(A.after(m).activation(best1_f[:, bass.ds(i * 32, 32)], tmp[:, 832:864], ACT.Copy))

        selected = []

        def select_experts(i, j):
            if j == 2:
                A.done(A.after(V.mark()).activation(tmp[:, 768:800], best1[:, bass.ds(i * 32, 32)], ACT.Copy))
                m = A.done(A.after().activation(tmp[:, 832:864], best1_f[:, bass.ds(i * 32, 32)], ACT.Copy))
                V.after(m)
                m = best_experts(idx[:, 1, bass.ds(i * 16, 16)])
                selected[:] = [Mark(m.sem, m.const + m.per * (NH - 1))]
                V.done(V.after().tensor_copy(gate[:, 1, bass.ds(i * 16, 16)], top))

        for t in range(NT):
            peer_pass(t, expert_u, dot(t), None if t else select_keys, 1 if t else 12, 0 if t else 3)
            g3 = heads(gate[:, t, :], NH)
            V.done(V.after().tensor_copy(st[:, 72:80].unsqueeze(2), g3[:, :, 0:1]))
            m = V.done(V.after().tensor_tensor(g3, g3, per_head(st[:, 72:80], NH, 16), ALU.subtract))
            m = A.done(A.after(m).activation(gate[:, t, :], gate[:, t, :], ACT.Exp))
            V.done(V.after(m).tensor_reduce(st[:, 56:64], g3, AX, ALU.add))
            V.done(V.after().reciprocal(st[:, 56:64], st[:, 56:64]))
            V.done(V.after().tensor_tensor(g3, g3, per_head(st[:, 56:64], NH, 16), ALU.mult))
            m = A.done(A.after(V.mark()).activation(act[:, t, :], act[:, t, :], ACT.Gelu_apprx_tanh))
            V.done(V.after(m).tensor_tensor(act[:, t, :], act[:, t, :], gate[:, t, :], ALU.mult))
            peer_pass(t, expert_v, add_row(t), None if t else select_experts, 1 if t else 20, 0 if t else 2)
            idx_ok[1] = selected[0]
        set_junk(rows_used.mark())

        V.done(V.after().tensor_copy(st[:, 95:96], st[:, 0:1]))
        enter_block(COLS["ple"], V.mark())
        sg = tmp[:, :].rearrange("p (t n) -> p t n", t=NT)

        def ple_body(i):
            for j in range(2):
                def f(banks, got):
                    cs = bass.ds(i * (2 * NC) + j * NC, NC)
                    before = V.mark()
                    for t in range(NT):
                        m = A.done(A.after(got, before).activation(sg[:, t, :], banks[t], ACT.Sigmoid, scale=st[:, RSTD + t:RSTD + t + 1]),
                                   evac if t else None)
                    for t in range(NT):
                        V.done(V.after(m).tensor_tensor(sg[:, t, :], sg[:, t, :], proj[:, t, cs], ALU.mult))
                        V.done(V.after().tensor_tensor(h[:, t, cs], h[:, t, cs], sg[:, t, :], ALU.add))
                dense(4, f)
        dense_loop(2, ple_body, 8, 2, {V.own: 8, A.own: 2})

        enter_block(COLS["norm2"], V.mark())
        B = w(0, NT, 7 * AW)
        V.after(T.mark())

        def in2_body(i):
            for j in range(2):
                dense(4, copy_out(lambda t: B[:, t, bass.ds(i * (2 * NC) + j * NC, NC)], RSTD))
        dense_loop(4, in2_body, 8, 2, {V.own: 2})
        ok = evac.mark()

        def gating_half():
            for n in range(8, 14):
                yield from dense_steps(4, copy_out(lambda t: B[:, t, n * NC:(n + 1) * NC], RSTD))
        side[0] = gating_half()

        def part2(t, s, n=1):
            return B[:, t, s * AW:(s + n) * AW]
        wsT = W[:, 18432:18432 + AW]
        ws_in = load("ws", wsT, w_spatial_t, V.mark())
        ws_ok = G.done(G.after(ws_in).affine_select(out=heads(wsT, 8), in_=heads(wsT, 8), compare_op=ALU.is_ge, fill=0.0,
                                                    base=0, pattern=[[0, 8], [1, 128]], channel_multiplier=-1))

        def norm_groups(ap, gain, ss, *marks):
            m = A.done(A.after(*marks, *junk_free()).activation(junk[:, 0:AW], ap, ACT.Square))
            m = V.done(V.after(m).tensor_reduce(ss, heads(junk[:, 0:AW], 8), AX, ALU.add))
            set_junk(m)
            rstd(ss, 128)
            V.done(V.after().tensor_tensor(heads(ap, 8), heads(ap, 8), per_head(ss, 8, 128), ALU.mult))
            return V.done(V.after().tensor_tensor(heads(ap, 8), heads(ap, 8), per_dim(row(gain, 128), 8, 128), ALU.mult))

        for t in range(NT):
            norm_groups(part2(t, 0), "q_norm2", st[:, 16:24], ok)
            tick()
            norm_groups(part2(t, 1), "k_norm2", st[:, 24:32])
            tick()
        for t in range(NT):
            silu_ok = A.done(A.after().activation(part2(t, 3), part2(t, 3), ACT.Silu))

        q2T, k2T = W[:, 14336:16384], W[:, 16384:18432]
        ok = V.mark()
        transposes(8, lambda t, k: part2(t, 0)[:, k * 128:(k + 1) * 128], to_plain(q2T), ok)
        transposes(8, lambda t, k: part2(t, 1)[:, k * 128:(k + 1) * 128], to_plain(k2T), ok)
        T.after(A.mark(), V.mark())
        prob2 = [B[:, 0, 0:1024].rearrange("p (k n) -> p k n", k=8), B[:, 1, 0:2048].rearrange("p (k n) -> p k n", k=8)]
        o2 = [part2(0, 0), part2(1, 0)]
        tp = tmp

        def causal_score(t):
            def f(k, o):
                return T.eng.matmul(o, q2T[:, k * S + t * 128:k * S + (t + 1) * 128], k2T[:, k * S:k * S + (t + 1) * 128], start=True, stop=True)
            return f
        V.after(T.mark())
        for t in range(NT):
            ok = softmax(8, (t + 1) * 128, 128 ** -0.5, t, causal_score(t), 1, prob2[t], st[:, 48 + 8 * t:56 + 8 * t], False, 3)
        pT2 = W[:, 14336:14336 + 3072].rearrange("p (k n) -> p k n", k=8)
        A.after(T.mark())
        V.after(T.mark())
        turn_probabilities(lambda t: prob2[t], lambda k: pT2[:, k, :], ok)
        T.after(A.mark(), V.mark())
        for t in range(NT):
            for g in range(2):
                b = 6 + g
                T.after(*bank_free[b])
                for j in range(4):
                    k = 4 * g + j
                    for kt_ in range(t + 1):
                        at = 0 if t == 0 else 128 + kt_ * 128
                        m = T.eng.matmul(ps[:, b, j * 128:(j + 1) * 128], pT2[:, k, at:at + 128], part2(kt_, 2)[:, k * 128:(k + 1) * 128],
                                         start=(kt_ == 0), stop=(kt_ == t))
                m = T.done(m)
                for j in range(4):
                    k = 4 * g + j
                    s = slice(k * 128, (k + 1) * 128)
                    m2 = V.done(V.after(m, silu_ok).scalar_tensor_tensor(o2[t][:, s], ps[:, b, j * 128:(j + 1) * 128],
                                                                         st[:, 48 + 8 * t + k:49 + 8 * t + k], part2(t, 3)[:, s], ALU.mult, ALU.mult))
                bank_free[b] = [m2]
                tick()
        side_done()
        side_ok = evac.mark()
        aTh, aTl = over("aTh", W_at, 14336, [8, S]), over("aTl", W_at, 16384, [8, S])
        A.after(T.mark())
        transposes(8, lambda t, k: o2[t][:, k * 128:(k + 1) * 128], to_split(aTh, aTl), V.mark())
        T.after(V.mark())

        merged = B[:, :, 2048:4096]
        sTh = over("sTh", W_at, 0, [8, S])
        sTl = over("sTl", W_at, 7 * AW, [8, S])

        def merge_steps(cs):
            def gated(banks, got):
                before = V.mark()
                for t in range(NT):
                    A.done(A.after(got, before).activation(sg[:, t, :], banks[t], ACT.Sigmoid, scale=st[:, RSTD + t:RSTD + t + 1]),
                           evac if t else None)

            def first(banks, got):
                V.done(V.after(got, evac.mark()).tensor_tensor(merged[:, 0, cs], banks[0], sg[:, 0, :], ALU.mult))
                V.done(V.after().tensor_tensor(merged[:, 1, cs], banks[1], sg[:, 1, :], ALU.mult), evac)
                V.done(V.after().tensor_copy(st[:, 95:96], st[:, 0:1]))

            def second(banks, got):
                V.done(V.after(got, evac.mark()).tensor_tensor(sg[:, 0, :], banks[0], sg[:, 0, :], ALU.mult))
                V.done(V.after().tensor_tensor(sg[:, 1, :], banks[1], sg[:, 1, :], ALU.mult), evac)
                for t in range(NT):
                    V.done(V.after().tensor_tensor(merged[:, t, cs], merged[:, t, cs], sg[:, t, :], ALU.add))
            yield from dense_steps(4, gated)
            yield from dense_steps(2, first, lhs=(aTh, aTl))
            yield from dense_steps(4, gated)
            yield from dense_steps(2, second, lhs=(sTh, sTl))
        side[0] = merge_steps(slice(0, NC))
        m = V.mark()
        tick()
        for t in range(NT):
            m = A.done(A.after(m, side_ok).activation(part2(t, 4, 2), part2(t, 4, 2), ACT.Gelu_apprx_tanh))
        tick()
        for t in range(NT):
            norm_groups(part2(t, 5), "sgu", st[:, 32:40], m)
            tick()
        T.after(V.mark())
        for t in range(NT):
            zb_ok = A.done(A.after().activation(part2(t, 6), part2(t, 6), ACT.Silu))
        T.after(ws_ok)
        for t in range(NT):
            for g in range(2):
                b = 6 + g
                T.after(*bank_free[b])
                for j in range(4):
                    k = 4 * g + j
                    m = T.eng.matmul(ps[:, b, j * 128:(j + 1) * 128], wsT[:, k * 128:(k + 1) * 128], part2(t, 5)[:, k * 128:(k + 1) * 128],
                                     start=True, stop=True)
                m = T.done(m)
                for j in range(4):
                    k = 4 * g + j
                    s = slice(k * 128, (k + 1) * 128)
                    bs = colv[:, COLS["b_spatial"] + k:COLS["b_spatial"] + k + 1]
                    m2 = V.done(V.after(m).scalar_tensor_tensor(part2(t, 4)[:, s], ps[:, b, j * 128:(j + 1) * 128], bs, part2(t, 4)[:, s], ALU.add, ALU.mult))
                bank_free[b] = [m2]
                tick()
            V.done(V.after(zb_ok).tensor_tensor(part2(t, 4), part2(t, 4), part2(t, 6), ALU.mult))
        A.after(T.mark())
        transposes(8, lambda t, k: part2(t, 4)[:, k * 128:(k + 1) * 128], to_split(sTh, sTl), V.mark())
        T.after(V.mark(), A.mark())

        side_done()
        dense_loop(3, lambda i: [None for _ in merge_steps(bass.ds(i * NC + NC, NC))], 12, 4, {V.own: 5, A.own: 2})
        A.after(used.mark())
        transposes(DK, lambda t, k: merged[:, t, k * 128:(k + 1) * 128], to_split(xh, xl), V.mark(), evac.mark())
        T.after(V.mark())
        for n in range(4):
            def f(banks, got):
                for t in range(NT):
                    o = h[:, t, n * NC:(n + 1) * NC]
                    m = V.done(V.after(got).tensor_tensor(o, banks[t], o, ALU.add), evac if t else None)
                for t in range(NT):
                    A.after(m).dma_start(out[t * 128:(t + 1) * 128, n * NC:(n + 1) * NC], h[:, t, n * NC:(n + 1) * NC]).then_inc(loads["out"], 16)
            dense(4, f, last=(n == 3))
        assert used.count == CHUNKS == split_at[0]
        nc.scalar.wait_ge(loads["out"], 16 * 4 * NT)


def blocks_of(wt):
    K, N = wt.shape
    return wt.reshape(K // 512, 4, 128, N // NC, NC).transpose(3, 0, 2, 1, 4).reshape(-1, 128, CW)


def kernel(**inputs):
    import concourse.bacc as bacc
    from concourse.bass_utils import run_bass_kernel_spmd

    a = {k: np.asarray(v) for k, v in inputs.items()}
    f32 = np.float32
    a = {k: (v if k in ("x", "positions", "p") else v[0]) for k, v in a.items()}
    w_in, w_in_2 = a["w_in"], a["w_in_2"]
    rope = np.zeros((128, CW), f32)
    rope[:, :DK * QR] = w_in[:, D:].reshape(DK, 128, QR).transpose(1, 0, 2).reshape(128, DK * QR)
    pool = a["w_pool"].reshape(4, 2, 128, 256).transpose(2, 0, 1, 3).reshape(1, 128, CW)
    keys = np.stack([a["sub_k1"], a["sub_k2"]], 1).transpose(3, 0, 1, 2).reshape(1, 128, CW)
    proj = a["w_ple_proj"].reshape(2, 128, 4, NC).transpose(1, 2, 0, 3).reshape(128, 2, CW).transpose(1, 0, 2)
    n = AW
    ga, gb = blocks_of(w_in_2[:, 7 * n:7 * n + D]), blocks_of(w_in_2[:, 7 * n + D:])
    pa, pb = blocks_of(a["w_proj_a_2"]), blocks_of(a["w_proj_b_2"])
    merge = [c for i in range(4) for c in (ga[4 * i:4 * i + 4], pa[2 * i:2 * i + 2], gb[4 * i:4 * i + 4], pb[2 * i:2 * i + 2])]
    weights = np.concatenate([blocks_of(w_in[:, :D]), rope[None], pool, blocks_of(a["w_uq"]), blocks_of(a["w_ukv"]),
                              blocks_of(a["w_out"][:POOL_W]), blocks_of(a["w_out"][POOL_W:]), keys, blocks_of(a["w_pq"]), proj, blocks_of(a["w_ple_gate"]),
                              blocks_of(w_in_2[:, :7 * n])] + merge + [blocks_of(a["w_out_2"])])

    def col(v):
        return v.reshape(-1, 128).T
    cols = np.concatenate([col(a["mix_norm_gain"]), col(a["ffn_norm_gain"]), col(a["ple_norm_gain"]), col(a["norm_g_2"]), col(a["pool_scale"]),
                           col(a["q_lat_gain"]), col(a["kv_lat_gain"]), a["b_spatial_2"].T], 1)
    inv_freq = (f32(10000.0) ** (-np.arange(0, QR, 2, dtype=f32) / f32(QR))).astype(f32)
    rows = np.concatenate([a["q_norm_gain"], a["k_norm_gain"], a["q_norm_g_2"], a["k_norm_g_2"], a["sgu_norm_g_2"],
                           inv_freq, np.arange(16, dtype=f32)])[None]
    pool_op = np.zeros((S, 4, S), f32)
    for g, win in enumerate(POOL_WINDOWS):
        for t in range(S):
            lo = max(0, t - win + 1)
            pool_op[lo:t + 1, g, t] = f32(1) / f32(t + 1 - lo)
            pool_op[t, g, t] -= f32(1)
    arrays = dict(
        x=a["x"][0], cols=cols, rows=rows, positions=a["positions"].reshape(NT, 128).T, ffn_gain=a["ffn_norm_gain"][None],
        pool_op=pool_op.reshape(NT, 128, 4 * S).transpose(1, 0, 2).reshape(128, NT * 4 * S),
        p_t=a["p"][0, 0].T.reshape(2, 128, S).transpose(1, 0, 2).reshape(128, 2 * S),
        w_spatial_t=a["w_spatial_2"].transpose(2, 0, 1).reshape(128, 8 * 128),
        weights=weights, expert_u=a["expert_u"], expert_v=a["expert_v"])
    arrays = {k: np.ascontiguousarray(v) for k, v in arrays.items()}
    nc = bacc.Bacc("TRN2", target_bir_lowering=False, num_devices=1)
    aps = {k: nc.dram_tensor("in_" + k, v.shape, mybir.dt.from_np(v.dtype), kind="ExternalInput").ap() for k, v in arrays.items()}
    out = nc.dram_tensor("out", (S, D), F32, kind="ExternalOutput").ap()
    build(nc, out=out, **aps)
    r = run_bass_kernel_spmd(nc, [{"in_" + k: v for k, v in arrays.items()}], core_ids=[0])
    return r.results[0]["out"].reshape(1, S, D)
```

```python
from contextlib import ExitStack, contextmanager

import numpy as np
import concourse.bass as bass
from concourse import mybir

F32, F32R = mybir.dt.float32, mybir.dt.float32r
I32, U32 = mybir.dt.int32, mybir.dt.uint32
ALU, ACT = mybir.AluOpType, mybir.ActivationFunctionType
AX = mybir.AxisListType.X
ENG = mybir.EngineType

P128 = 128
S = 256
NT = S // P128
D = 2048
DK = D // P128
EPS = 1e-6
POOL_W, POOL_WINDOWS = 1024, (2, 4, 8, 16)
NH, QN, QR, LORA = 8, 128, 64, 512
QH = QN + QR
CHUNK = 64
NKEYS = 128
AW = 1024
CW = 2048
NC = 512
RAW = 4
SPL = 2
GR = 8
SCHEDULE = (["d", "", "", "d", "", "", "", "d", "", "d", "", "s", "s"],
            ["dr", "r", "dr", "r", "r", "dr", "r", "dr", "r", "r", "sr", "r", "s"],
            ["dr", "r", "dr", "r", "r", "dr", "r", "dr", "r", "r", "sr", "r", "s"],
            ["p"] + ["r"] * 12)
EARLY = 2
NEG = -1e30

N_CHUNKS = dict(w_in=16, w_rope=1, w_pool=1, w_uq=3, w_ukv=4, w_out=16, sub_k=1, w_pq=16, ple_proj=2, ple_gate=16,
                w_in_2=56, merge=48, w_out_2=16)
CHUNKS = sum(N_CHUNKS.values())

COLS, _at = {}, 0
for _n, _w in (("mix", 16), ("ffn", 16), ("ple", 16), ("norm2", 16), ("pool_scale", 8), ("q_lat", 4), ("kv_lat", 4),
               ("b_spatial", 8), ("q_nope", 1), ("k_nope", 1)):
    COLS[_n] = _at
    _at += _w
N_COLS = _at
ROWS, _at = {}, 0
for _n, _w in (("q_norm", QH), ("k_norm", QH), ("q_norm2", 128), ("k_norm2", 128), ("sgu", 128), ("inv_freq", 32),
               ("iota", 16)):
    ROWS[_n] = _at
    _at += _w
N_ROWS = _at


class Mark:
    def __init__(self, sem, const, per=0, i=None):
        self.sem, self.const, self.per, self.i = sem, const, per, i

    def value(self):
        return self.const if self.i is None or not self.per else self.i * self.per + self.const


class Counter:
    def __init__(self, sem, count=0):
        self.sem, self.count, self.start, self.per, self.i = sem, count, count, 0, None

    def mark(self, back=0):
        return Mark(self.sem, self.count - back, self.per, self.i)


class Lane:
    def __init__(self, eng, sem, chained=True):
        self.eng, self.own, self.chained, self.last = eng, Counter(sem), chained, []
        self.counters = [self.own]

    def after(self, *marks):
        for m in list(marks) + (self.last if self.chained else []):
            self.eng.wait_ge(m.sem, m.value())
        return self.eng

    def only(self, *marks):
        for m in marks:
            self.eng.wait_ge(m.sem, m.value())
        return self.eng

    def done(self, ins, counter=None):
        c = counter or self.own
        ins.then_inc(c.sem, 1)
        c.count += 1
        self.last = [c.mark()]
        return c.mark()

    def mark(self):
        return self.own.mark()


def build(nc, x, cols, rows, positions, ffn_gain, pool_op, p_t, w_spatial_t, weights, expert_u, expert_v, out):
    with ExitStack() as ctx:
        def sb(name, shape, dt=F32):
            return ctx.enter_context(nc.sbuf_tensor(name, shape, dt))

        def sem(name):
            return ctx.enter_context(nc.semaphore(name))

        def placed():
            return -(-nc.sbuf_base // 32) * 32

        def over(name, base, at, shape, dt=F32R):
            return nc.alloc_sbuf_tensor_at(name, [128] + shape, dt, offset=base + 4 * at)

        raw = sb("raw", [128, RAW, CW])
        whi = sb("whi", [128, SPL, CW], F32R)
        wlo = sb("wlo", [128, SPL, CW], F32R)
        xT_at = placed()
        xT = sb("xT", [128, 2, DK * S], F32R)
        h = sb("h", [128, NT, D])
        W_at = placed()
        W = sb("W", [128, 20736])
        colv = sb("colv", [128, N_COLS])
        rowv = sb("rowv", [128, N_ROWS])
        ident = sb("ident", [128, 128])
        mask = sb("mask", [128, 2, 256])
        tmp = sb("tmp", [128, 1024])
        pos = sb("pos", [128, NT], I32)
        trig = sb("trig", [128, 2, NT, 32])
        st = sb("st", [128, 96])
        idx = sb("idx", [128, NT, 128], I32)
        gate = sb("gate", [128, NT, 128])
        act = sb("act", [128, NT, 128])
        idx_now = sb("idx_now", [128, 16], I32)
        col_now = sb("col_now", [128, 16])
        ps = ctx.enter_context(nc.psum_tensor("ps", [128, 8, 512], F32))

        xh = xT[:, 0, :].rearrange("p (k s) -> p k s", k=DK)
        xl = xT[:, 1, :].rearrange("p (k s) -> p k s", k=DK)

        def w(at, *shape):
            n = int(np.prod(shape))
            v = W[:, at:at + n]
            if len(shape) == 2:
                v = v.rearrange("p (a b) -> p a b", a=shape[0])
            elif len(shape) == 3:
                v = v.rearrange("p (a b c) -> p a b c", a=shape[0], b=shape[1])
            return v

        def row(name, n):
            return rowv[:, ROWS[name]:ROWS[name] + n]

        V = Lane(nc.vector, sem("v_done"))
        A = Lane(nc.scalar, sem("a_done"))
        T = Lane(nc.tensor, sem("t_done"), chained=False)
        G = Lane(nc.gpsimd, sem("p_done"))
        hi_done = Counter(sem("hi_done"))
        lo_done = Counter(sem("lo_done"))
        used = Counter(sem("used"))
        evac = Counter(sem("evac"))
        rows_used = Counter(sem("rows_used"), GR)
        A.counters += [hi_done, evac]
        V.counters += [lo_done, evac, rows_used]
        T.counters += [used]
        landed = [sem(f"landed{r}") for r in range(RAW)]
        row_in = [sem(f"row_in{r}") for r in range(GR)]
        early_in = [sem(f"early_in{r}") for r in range(2)]
        loads = {n: sem("load_" + n) for n in ("x", "cols", "rows", "pos", "pool_op", "p", "ffn", "ws", "out")}
        everything = [V.own, A.own, T.own, G.own, hi_done, lo_done, used, evac, rows_used]

        @contextmanager
        def loop(n, per, lanes):
            base = {c: c.count for c in everything}
            with nc.Fori(0, n, engines=[{V: ENG.DVE, A: ENG.Activation, T: ENG.PE, G: ENG.Pool}[k] for k in lanes]) as i:
                for c, k in per.items():
                    c.per, c.i = k, i
                for k in lanes:
                    k.last = [c.mark() for c in k.counters if c.count != c.start or c in per]
                yield i
                got = {c: c.count - base[c] for c in everything if c.count != base[c]}
                assert got == per, sorted((c.sem.name, v) for c, v in got.items())
            for c, k in per.items():
                c.per, c.i, c.count = 0, None, base[c] + k * n
            for k in lanes:
                k.last = [c.mark() for c in k.counters if c.count != c.start or c in per]

        def load(name, dst, src, *marks):
            for m in marks:
                nc.scalar.wait_ge(m.sem, m.value())
            nc.scalar.dma_start(dst, src).then_inc(loads[name], 16)
            return Mark(loads[name], 16)

        for t in range(NT):
            nc.sync.dma_start(h[:, t, :], x[t * 128:(t + 1) * 128, :]).then_inc(loads["x"], 16)
        x_in = Mark(loads["x"], 16 * NT)
        for c in range(RAW):
            nc.sync.dma_start(raw[:, c, :], weights[c]).then_inc(landed[c], 16)
        assert CHUNKS % RAW == 0
        with nc.Fori(0, CHUNKS // RAW - 1, engines=[ENG.SP]) as g:
            for r in range(RAW):
                nc.sync.wait_ge(used.sem, g * RAW + (r + 1))
                nc.sync.dma_start(raw[:, r, :], weights[bass.ds(g * RAW + (RAW + r), 1)].rearrange("a p n -> p (a n)"))\
                    .then_inc(landed[r], 16)

        cols_in = load("cols", colv[:, :], cols)
        rows_in = load("rows", rowv[:, :], rows.broadcast_to([128, N_ROWS]))
        pos_in = load("pos", pos[:, :], positions)
        POOL_OP = w(15488, 2, 4, 256)
        pool_in = load("pool_op", W[:, 15488:15488 + 2048], pool_op)

        G.done(G.after().memset(tmp[:, 0:128], 1.0))
        ident_ok = G.done(G.after().affine_select(out=ident[:, :], in_=tmp[:, 0:128], compare_op=ALU.is_equal, fill=0.0,
                                                  base=0, pattern=[[-1, 128]], channel_multiplier=1))
        G.done(G.after().memset(mask[:, :, :], 0.0))
        G.done(G.after().memset(mask[0:CHUNK, 0, 128 + CHUNK:256], NEG))
        mask_ok = G.done(G.after().affine_select(out=mask[:, 1, 128:256], in_=mask[:, 1, 128:256], compare_op=ALU.is_ge,
                                                 fill=NEG, base=0, pattern=[[-1, 128]], channel_multiplier=1))
        T.after(ident_ok)
        V.after(cols_in, rows_in)
        A.after(cols_in)

        split_at = [0]
        kept_at = {}

        def split_next():
            c = split_at[0]
            r, b = c % RAW, c % SPL
            per = hi_done.per
            here = Mark(landed[r], 16 * (c // RAW + 1), 16 * per // RAW if per else 0, hi_done.i)
            free = [Mark(used.sem, c - SPL + 1, per, hi_done.i)] if c >= SPL else []
            hi_at, lo_at = kept_at.get(c, (whi[:, b, :], wlo[:, b, :]))
            hi = A.done(A.after(here, *free).activation(hi_at, raw[:, r, :], ACT.Copy), hi_done)
            V.done(V.after(hi).tensor_tensor(lo_at, raw[:, r, :], hi_at.bitcast(F32), ALU.subtract), lo_done)
            split_at[0] += 1

        def next_chunk(last=False):
            c = used.count
            if not last:
                split_next()
            T.after(Mark(lo_done.sem, c + 1, used.per, used.i))
            return whi[:, c % SPL, :], wlo[:, c % SPL, :]

        def products(out_ap, a, b, start, stop):
            T.eng.matmul(out_ap, a[0], b[0], start=start, stop=False)
            T.eng.matmul(out_ap, a[0], b[1], start=False, stop=False)
            return T.eng.matmul(out_ap, a[1], b[0], start=False, stop=stop)

        pairs = [0]

        def dense_steps(n_q, evacuate, q0=0, cols_n=NC, lhs=None, last=False, ready=None, then=None):
            lh, ll = lhs or (xh, xl)
            pair = 2 * (pairs[0] % 2)
            if pairs[0] >= 2:
                T.after(Mark(evac.sem, pairs[0] - 1, evac.per, evac.i))
            pairs[0] += 1
            for q in range(n_q):
                hi, lo = next_chunk(last=last and q == n_q - 1)
                nk = min(CW // cols_n, 4 if cols_n == NC else DK)
                if ready:
                    T.after(ready[q])
                for k in range(nk):
                    for t in range(NT):
                        o = ps[:, pair + t, 0:cols_n]
                        s = slice(t * 128, (t + 1) * 128)
                        cs = slice(k * cols_n, (k + 1) * cols_n)
                        ks = q0 + q * 4 + k
                        m = products(o, (lh[:, ks, s], ll[:, ks, s]), (hi[:, cs], lo[:, cs]),
                                     start=(q == 0 and k == 0), stop=(q == n_q - 1 and k == nk - 1))
                got = T.done(m, used)
                if then and q in then:
                    then[q]()
                if q < n_q - 1:
                    yield
            evacuate([ps[:, pair + t, 0:cols_n] for t in range(NT)], got)
            yield

        def dense(*args, **kw):
            for _ in dense_steps(*args, **kw):
                pass

        side = [iter(())]

        def tick(n=1):
            for _ in range(n):
                next(side[0], None)

        def side_done():
            for _ in side[0]:
                pass

        def dense_loop(n, body, chunks, blocks, per):
            assert chunks % RAW == 0 and blocks % 2 == 0
            c0, p0 = split_at[0], pairs[0]
            full = {hi_done: chunks, lo_done: chunks, used: chunks, evac: blocks}
            full.update(per)
            with loop(n, full, [V, A, T]) as i:
                body(i)
            split_at[0], pairs[0] = c0 + n * chunks, p0 + n * blocks

        def copy_out(dst, scale=None, lane=V):
            def f(banks, got):
                for t in range(NT):
                    e = lane.after(got)
                    if lane is A:
                        ins = e.activation(dst(t), banks[t], ACT.Copy, scale=st[:, scale + t:scale + t + 1])
                    elif scale is None:
                        ins = e.tensor_copy(dst(t), banks[t])
                    else:
                        ins = e.tensor_scalar(dst(t), banks[t], st[:, scale + t:scale + t + 1], None, ALU.mult)
                    lane.done(ins, evac if t else None)
            return f

        bank_free = {b: [] for b in range(8)}

        def transposes(n, src, put, *marks, first=0):
            T.after(*marks)
            for g in range(first // 2, (first + n) // 2):
                b = 4 + g % 4
                T.after(*bank_free[b])
                for k in range(2):
                    for t in range(NT):
                        m = T.eng.transpose(ps[:, b, (2 * k + t) * 128:(2 * k + t + 1) * 128], src(t, 2 * g + k), ident[:, :])
                bank_free[b] = put(g, ps[:, b, :], T.done(m))

        def two(ap, g):
            return ap[:, 2 * g:2 * g + 2, :].rearrange("p k s -> p (k s)")

        def to_split(hi, lo, gain=None):
            def put(g, bank, got):
                if gain is None:
                    m = A.done(A.after(got).activation(two(hi, g), bank, ACT.Copy))
                    m = V.done(V.after(m).tensor_tensor(two(lo, g), bank, two(hi, g).bitcast(F32), ALU.subtract))
                else:
                    s = [colv[:, gain + 2 * g + k:gain + 2 * g + k + 1] for k in range(2)]
                    for k in range(2):
                        m = A.done(A.after(got).activation(hi[:, 2 * g + k, :], bank[:, k * S:(k + 1) * S], ACT.Copy, scale=s[k]))
                    for k in range(2):
                        m = V.done(V.after(m).scalar_tensor_tensor(lo[:, 2 * g + k, :], bank[:, k * S:(k + 1) * S], s[k],
                                                                   hi[:, 2 * g + k, :].bitcast(F32), ALU.mult, ALU.subtract))
                return [m]
            return put

        def to_plain(dst, gain=None):
            s = 1.0 if gain is None else colv[:, gain:gain + 1]

            def put(g, bank, got):
                if g % 2:
                    return [A.done(A.after(got).activation(dst[:, g * 512:(g + 1) * 512], bank, ACT.Copy, scale=s))]
                if gain is not None:
                    return [V.done(V.after(got).tensor_scalar(dst[:, g * 512:(g + 1) * 512], bank, s, None, ALU.mult))]
                return [V.done(V.after(got).tensor_copy(dst[:, g * 512:(g + 1) * 512], bank))]
            return put

        def rstd(ss, n, *marks):
            m = V.done(V.after(*marks).tensor_scalar(ss, ss, 1.0 / n, EPS, ALU.mult, ALU.add))
            m = A.done(A.after(m).activation(ss, ss, ACT.Sqrt))
            return V.done(V.after(m).reciprocal(ss, ss))

        RSTD = 0

        def square_rows(t):
            m = A.done(A.after(V.mark(), *[m for b in range(4, 8) for m in bank_free[b]])
                       .activation(ps[:, 4:8, :].rearrange("p a b -> p (a b)"), h[:, t, :], ACT.Square, accum_out=st[:, RSTD + t:RSTD + t + 1]))
            for b in range(4, 8):
                bank_free[b] = [m]

        def row_rstd():
            A.after(rstd(st[:, RSTD:RSTD + NT], D, A.mark()))

        class Entry:
            def __init__(self, src, gain=None):
                self.src, self.gain, self.ready = src, gain, {}

            def part(self, q, *marks):
                A.after(used.mark())
                transposes(4, self.src, to_split(xh, xl, self.gain), *marks, first=4 * q)
                self.ready[q] = V.mark()

            def later(self, q, *marks):
                return lambda: self.part(q, *marks)

            def rest(self, *marks):
                return {1: lambda: (self.part(3, *marks), square_rows(0)), 2: lambda: square_rows(1), 3: row_rstd}

        def stream_entry(gain):
            return Entry(lambda t, k: h[:, t, k * 128:(k + 1) * 128], gain)

        def angles():
            TWO_PI = 2 * np.pi
            C1 = 6.28125
            C2 = float(np.float32(np.round((TWO_PI - C1) * 2 ** 19) / 2 ** 19))
            C3 = float(TWO_PI - C1 - C2)
            ang, turns = tmp[:, 256:320].rearrange("p (t f) -> p t f", t=NT), tmp[:, 320:384].rearrange("p (t f) -> p t f", t=NT)
            V.done(V.after(pos_in, A.mark()).tensor_copy(st[:, 8:8 + NT], pos[:, :]))
            for t in range(NT):
                V.done(V.after().tensor_scalar(ang[:, t, :], row("inv_freq", 32), st[:, 8 + t:9 + t], None, ALU.mult))
            V.done(V.after().tensor_scalar(turns, ang, 1.0 / TWO_PI, 12582912.0, ALU.mult, ALU.add))
            V.done(V.after().tensor_scalar(turns, turns, 12582912.0, None, ALU.subtract))
            for c in (C1, C2, C3):
                V.done(V.after().scalar_tensor_tensor(ang, turns, -c, ang, ALU.mult, ALU.add))
            V.done(V.after().tensor_scalar(trig[:, 1, :, :], ang, 3.1415925, -3.1415925, ALU.min, ALU.max))
            V.done(V.after().tensor_scalar(ang, ang, float(np.pi / 2), None, ALU.add))
            V.done(V.after().tensor_scalar(turns, ang, float(np.pi), -TWO_PI, ALU.is_gt, ALU.mult))
            V.done(V.after().tensor_tensor(ang, ang, turns, ALU.add))
            m = V.done(V.after().tensor_scalar(trig[:, 0, :, :], ang, 3.1415925, -3.1415925, ALU.min, ALU.max))
            return A.done(A.after(m).activation(trig[:, :, :, :], trig[:, :, :, :], ACT.Sin))

        into = stream_entry(COLS["mix"])
        into.part(0, x_in)
        split_next()
        into.part(1)
        Z_W = D + QR
        z = w(0, NT, Z_W)

        for n in range(4):
            then = {0: into.later(2), **into.rest()} if n == 0 else None
            dense(4, copy_out(lambda t: z[:, t, n * NC:(n + 1) * NC], RSTD), ready=into.ready if n == 0 else None, then=then)
            if n == 1:
                trig_ok = angles()
        lat_in = evac.mark()
        dense(1, copy_out(lambda t: z[:, t, D:Z_W], RSTD), cols_n=QR)
        z_ok = evac.mark()

        A.after(used.mark())
        transposes(8, lambda t, k: z[:, t, POOL_W + k * 128:POOL_W + (k + 1) * 128],
                   to_split(xh[:, 8:16, :], xl[:, 8:16, :], COLS["q_lat"]), lat_in)
        lat_ok = V.mark()

        dTh, dTl = over("dTh", W_at, 11392, [8, S]), over("dTl", W_at, 13440, [8, S])
        T.after(z_ok, pool_in)
        for k in range(8):
            b = 4 + k % 4
            T.after(*bank_free[b])
            for t in range(NT):
                m = T.eng.matmul(ps[:, b, 0:S], z[:, t, k * 128:(k + 1) * 128], POOL_OP[:, t, k // 2, :], start=(t == 0), stop=(t == 1))
            m = A.done(A.after(T.done(m)).activation(dTh[:, k, :], ps[:, b, 0:S], ACT.Copy))
            bank_free[b] = [V.done(V.after(m).tensor_tensor(dTl[:, k, :], ps[:, b, 0:S], dTh[:, k, :].bitcast(F32), ALU.subtract))]

        for j in range(2):
            for t in range(NT):
                c = POOL_W + j * LORA
                m = A.done(A.after(z_ok).activation(tmp[:, 0:LORA], z[:, t, c:c + LORA], ACT.Square, accum_out=st[:, 4 + 2 * j + t:5 + 2 * j + t]))
        rstd(st[:, 4:8], LORA, m)

        T.after(V.mark())
        phi, plo = next_chunk()
        for k in range(8):
            b = 4 + k % 4
            g, half = k // 2, k % 2
            T.after(*bank_free[b])
            for c in range(2):
                col = (g * 2 + c) * 256 + half * 128
                m = products(ps[:, b, 0:S], (phi[:, col:col + 128], plo[:, col:col + 128]), (dTh[:, 2 * g + c, :], dTl[:, 2 * g + c, :]),
                             start=(c == 0), stop=(c == 1))
            m = T.done(m, used if k == 7 else None)
            s = colv[:, COLS["pool_scale"] + k:COLS["pool_scale"] + k + 1]
            m = A.done(A.after(m).activation(xh[:, k, :], ps[:, b, 0:S], ACT.Copy, scale=s))
            bank_free[b] = [V.done(V.after(m).scalar_tensor_tensor(xl[:, k, :], ps[:, b, 0:S], s, xh[:, k, :].bitcast(F32), ALU.mult, ALU.subtract))]

        q = w(4224, NT, NH * QH)
        kv = w(7296, NT, NH * 256)
        T.after(lat_ok)
        for n in range(3):
            dense(1, copy_out(lambda t: q[:, t, n * NC:(n + 1) * NC], 4), q0=8)
        q_ok = evac.mark()
        for n in range(4):
            dense(1, copy_out(lambda t: kv[:, t, n * NC:(n + 1) * NC], 6), q0=12)

        kv_ok = evac.mark()

        def residual_in(at):
            def f(banks, got):
                for t in range(NT):
                    V.done(V.after(got).tensor_tensor(h[:, t, at], banks[t], h[:, t, at], ALU.add), evac if t else None)
            return f

        def pool_half():
            for n in range(4):
                yield from dense_steps(2, residual_in(slice(n * NC, (n + 1) * NC)))
        T.after(V.mark())
        side[0] = pool_half()

        def heads(ap, n):
            return ap.rearrange("p (h d) -> p h d", h=n)

        def per_head(ap, n, d):
            return ap.unsqueeze(2).broadcast_to([128, n, d])

        def per_dim(ap, n, d):
            return ap.unsqueeze(1).broadcast_to([128, n, d])

        junk = ps[:, 4:8, :].rearrange("p a b -> p (a b)")

        def junk_free():
            return [m for b in range(4, 8) for m in bank_free[b]]

        def set_junk(m):
            for b in range(4, 8):
                bank_free[b] = [m]

        qrh = w(18560, NT, NH * QR)
        krh = w(19584, NT, NH * QR)
        rot_a = tmp[:, 256:512]
        rot_b = tmp[:, 512:768]

        def rotate(dst, src, t, n):
            half = QR // 2
            cos, sin = per_dim(trig[:, 0, t, :], n, half), per_dim(trig[:, 1, t, :], n, half)
            a, b = heads(rot_a[:, 0:n * half], n), heads(rot_b[:, 0:n * half], n)
            x1, x2 = src[:, :, 0:half], src[:, :, half:QR]
            for o, (u, v_), op in ((dst[:, :, 0:half], (x1, x2), ALU.subtract), (dst[:, :, half:QR], (x2, x1), ALU.add)):
                V.done(V.after(trig_ok).tensor_tensor(a, u, cos, ALU.mult))
                V.done(V.after().tensor_tensor(b, v_, sin, ALU.mult))
                m = V.done(V.after().tensor_tensor(o, a, b, op))
            return m

        def squares(rows_, n, ss, *marks):
            A.after(*marks, *junk_free())
            for k in range(NH):
                m = A.done(A.after().activation(junk[:, 0:n], rows_[:, k, 0:n], ACT.Square, accum_out=ss[:, k:k + 1]))
            set_junk(m)
            return m

        for t in range(NT):
            qt = heads(q[:, t, :], NH)
            ss = st[:, 16 + 16 * t:24 + 16 * t]
            rstd(ss, QH, squares(qt, QH, ss, q_ok))
            V.done(V.after().tensor_tensor(qt, qt, per_head(ss, NH, QH), ALU.mult))
            V.done(V.after().tensor_tensor(qt[:, :, QN:QH], qt[:, :, QN:QH], per_dim(row("q_norm", QH)[:, QN:QH], NH, QR), ALU.mult))
            rotate(heads(qrh[:, t, :], NH), qt[:, :, QN:QH], t, NH)
            tick()
            kt = heads(kv[:, t, :], NH)
            kr = z[:, t, D:Z_W]
            ss, kr_ss = st[:, 24 + 16 * t:32 + 16 * t], st[:, 10 + t:11 + t]
            squares(kt, QN, ss, kv_ok)
            m = A.done(A.after().activation(junk[:, 0:QR], kr, ACT.Square, accum_out=kr_ss))
            set_junk(m)
            V.done(V.after(m).tensor_scalar(ss, ss, kr_ss, None, ALU.add))
            rstd(ss, QH)
            V.done(V.after().tensor_tensor(kt[:, :, 0:QN], kt[:, :, 0:QN], per_head(ss, NH, QN), ALU.mult))
            kg, kr2 = tmp[:, 128:192], tmp[:, 192:256]
            V.done(V.after().tensor_tensor(kg, kr, row("k_norm", QH)[:, QN:QH], ALU.mult))
            rotate(kr2.unsqueeze(1), kg.unsqueeze(1), t, 1)
            V.done(V.after().tensor_tensor(heads(krh[:, t, :], NH), per_dim(kr2, NH, QR), per_head(ss, NH, QR), ALU.mult))
            tick()

        qT, qrT = W[:, 11392:13440], W[:, 13440:14464]
        kT, krT = W[:, 0:2048], W[:, 2048:3072]
        A.after(T.mark(), used.mark())
        V.after(T.mark(), used.mark())
        ok = V.mark()
        transposes(NH, lambda t, k: q[:, t, k * QH:k * QH + QN], to_plain(qT, COLS["q_nope"]), ok)
        transposes(NH, lambda t, k: kv[:, t, k * 256:k * 256 + QN], to_plain(kT, COLS["k_nope"]), ok)
        transposes(NH // 2, lambda t, k: qrh[:, t, k * 128:(k + 1) * 128], to_plain(qrT), ok)
        transposes(NH // 2, lambda t, k: krh[:, t, k * 128:(k + 1) * 128], to_plain(krT), ok)

        def softmax(n_heads, n_keys, scale, t, score, which, p_out, sums, normed, ticks=0):
            per = 2
            for g in range(n_heads // per):
                b = 6 + g % 2
                T.after(*bank_free[b])
                k = 4 * (g // 2) + g % 2
                for j in range(per):
                    m = score(k + 2 * j, ps[:, b, j * n_keys:(j + 1) * n_keys])
                src = ps[:, b, 0:per * n_keys].rearrange("p (a k) -> p a k", a=per)
                dst = p_out[:, k:k + 3:2, :]
                msk = per_dim(mask[:, which, 256 - n_keys:256], per, n_keys)
                m = V.done(V.after(T.done(m), mask_ok).tensor_tensor(dst, src, msk, ALU.add))
                bank_free[b] = [m]
                if g % 2:
                    tick()
            mx = st[:, 40:48] if t == 0 else st[:, 80:88]
            V.done(V.after().tensor_reduce(mx, p_out, AX, ALU.max))
            nm = V.done(V.after(A.mark()).tensor_scalar(mx, mx, -scale, None, ALU.mult))
            for k in range(n_heads):
                m = A.done(A.after(nm).activation(p_out[:, k, :], p_out[:, k, :], ACT.Exp, bias=mx[:, k:k + 1], scale=scale,
                                                  accum_out=sums[:, k:k + 1]))
            tick(ticks // 2)
            yield m
            m = V.done(V.after(m).reciprocal(sums, sums))
            tick(ticks - ticks // 2)
            if normed:
                m = V.done(V.after().tensor_tensor(p_out, p_out, per_head(sums, n_heads, n_keys), ALU.mult))
            yield m

        def both_tiles(a, b):
            next(a), next(b)
            next(a)
            return next(b)

        def turn_probabilities(p_of, dst_of, ok):
            for k in range(NH):
                b = 4 + k % 4
                T.after(ok, *bank_free[b])
                for j, (t, kt_) in enumerate(((0, 0), (1, 0), (1, 1))):
                    m = T.eng.transpose(ps[:, b, j * 128:(j + 1) * 128], p_of(t)[:, k, kt_ * 128:(kt_ + 1) * 128], ident[:, :])
                m = T.done(m)
                if k % 4 == 3:
                    tick()
                if k % 2:
                    bank_free[b] = [V.done(V.after(m).tensor_copy(dst_of(k), ps[:, b, 0:384]))]
                else:
                    bank_free[b] = [A.done(A.after(m).activation(dst_of(k), ps[:, b, 0:384], ACT.Copy))]

        prob = [w(15488, NH, 128), w(16512, NH, 256)]
        pT = w(4224, NH, 384)
        T.after(A.mark(), V.mark())

        def mla_score(t):
            def f(k, o):
                keys, qs = (t + 1) * 128, slice(t * 128, (t + 1) * 128)
                T.eng.matmul(o, qT[:, k * S:(k + 1) * S][:, qs], kT[:, k * S:k * S + keys], start=True, stop=False)
                r = slice(64 * (k % 2), 64 * (k % 2) + 64)
                at = (k // 2) * S
                return T.eng.matmul(o, qrT[r, at:at + S][:, qs], krT[r, at:at + keys], start=False, stop=True)
            return f

        ok = both_tiles(*[softmax(NH, (t + 1) * 128, QH ** -0.5, t, mla_score(t), 0, prob[t], st[:, 48 + 8 * t:56 + 8 * t], True)
                          for t in range(NT)])
        V.after(T.mark())
        A.after(T.mark())
        turn_probabilities(lambda t: prob[t], lambda k: pT[:, k, :], ok)
        T.after(A.mark(), V.mark())
        for g in range(NH // 2):
            b = 6 + g % 2
            T.after(*bank_free[b])
            for j in range(2):
                k = 2 * g + j
                v_of = [kv[:, kt_, k * 256 + QN:(k + 1) * 256] for kt_ in range(2)]
                T.eng.matmul(ps[:, b, j * S:j * S + 128], v_of[0], pT[:, k, 0:128], start=True, stop=True)
                for kt_ in range(2):
                    m = T.eng.matmul(ps[:, b, j * S + 128:(j + 1) * S], v_of[kt_], pT[:, k, 128 + kt_ * 128:256 + kt_ * 128],
                                     start=(kt_ == 0), stop=(kt_ == 1))
            bank_free[b] = to_split(xh[:, 8:16, :], xl[:, 8:16, :])(g, ps[:, b, :], T.done(m))
        T.after(V.mark())

        side_done()

        KH, KL = over("KH", W_at, 16384, [CW]), over("KL", W_at, 18432, [CW])
        kept_at[used.count + 8] = (KH[:, :], KL[:, :])
        A.after(T.mark(), V.mark())
        into = stream_entry(COLS["ffn"])
        for n in range(4):
            ok = evac.mark()
            dense(2, residual_in(slice(n * NC, (n + 1) * NC)), q0=8, then={0: into.later(n - 1, ok)} if n else None)

        xn = w(0, NT, D)
        ffn_row = W[:, 14336:14336 + D]
        ffn_in = load("ffn", ffn_row, ffn_gain.broadcast_to([128, D]), V.mark(), T.mark(), A.mark(), evac.mark())
        p_in = load("p", w(10752, 2, S), p_t.rearrange("p (k s) -> p k s", k=2))
        next_chunk()
        T.after(*bank_free[4])
        T.done(T.eng.transpose(ps[:, 4, 0:128], ident[:, :], ident[:, :]), used)
        stream_ok = evac.mark()

        qb = w(4096, NT, NC)
        qh, ql = over("qh", W_at, 6144, [4, S]), over("ql", W_at, 7168, [4, S])
        s0 = [W[:, 5120:5120 + NC], W[:, 8192:8192 + NC]]
        s1 = W[:, 12288:12288 + D]

        def queries():
            for n in range(4):
                yield from dense_steps(4, copy_out(lambda t: qb[:, t, :], RSTD, A), ready=into.ready if n == 0 else None,
                                       then=into.rest(stream_ok) if n == 0 else None)
        pTs = w(10752, 2, S)
        pTh, pTl = over("pTh", W_at, 11264, [2, S]), over("pTl", W_at, 11776, [2, S])
        side[0] = queries()
        tick(4)

        between = [lambda: None]

        def top16(sets):
            last = [s[3] for s in sets]
            steps = [lambda v, o, i: V.eng.max(o[:, 0:8], v),
                     lambda v, o, i: V.eng.max_index(i[:, 0:8], o[:, 0:8], v),
                     lambda v, o, i: V.eng.match_replace(v, o[:, 0:8], v, -3.0e38),
                     lambda v, o, i: V.eng.max(o[:, 8:16], v),
                     lambda v, o, i: V.eng.max_index(i[:, 8:16], o[:, 8:16], v)]
            for r, step in enumerate(steps):
                between[0]()
                for n, (v, o, i, _) in enumerate(sets):
                    V.only(*last[n])
                    if V.own.i is not None:
                        V.eng.nop(nofuse=True)
                    last[n] = [V.done(step(v, o, i))]
            return V.mark()

        class Selection:
            def __init__(self, nh, at):
                self.nh = nh
                def piece(size, *shape):
                    nonlocal at
                    at += nh * size
                    v = tmp[:, at - nh * size:at]
                    if len(shape) == 2:
                        return v.rearrange("p (h a b) -> p h a b", a=shape[0], b=shape[1])
                    return v.rearrange("p (h a) -> p h a", h=nh)
                self.cand = piece(256, 16, 16)
                self.best, self.best_u, self.best_f = (piece(32, 2, 16) for _ in range(3))
                self.top, self.top_u = piece(16), piece(16)
                self.part_u = [piece(16).bitcast(U32) for _ in range(2)]
                self.part_f = [piece(16) for _ in range(2)]
                self.e_f = [piece(16) for _ in range(2)]
                self.best_u, self.top_u = self.best_u.bitcast(U32), self.top_u.bitcast(U32)

            def keys(self, scores, *marks):
                marks = [*marks, *V.last]
                top16([(scores[:, k, j, :], self.best[:, k, j, :], self.best_u[:, k, j, :], marks)
                       for k in range(self.nh) for j in range(2)])
                return V.done(V.after().tensor_copy(self.best_f, self.best_u))

            def experts(self, idx_out):
                nh, cand = self.nh, self.cand
                shape = [128, nh, 16, 16]
                for k in range(nh):
                    V.done(V.after().tensor_tensor(cand[:, k], self.best[:, k, 0, :].unsqueeze(2).broadcast_to([128, 16, 16]),
                                                   self.best[:, k, 1, :].unsqueeze(1).broadcast_to([128, 16, 16]), ALU.add))
                between[0]()
                top16([(cand[:, k].rearrange("p a b -> p (a b)"), self.top[:, k, :], self.top_u[:, k, :], V.last) for k in range(nh)])
                m = V.mark()
                V.done(V.only(m).tensor_scalar(self.part_u[0], self.top_u, 4, None, ALU.logical_shift_right))
                V.done(V.only(m).tensor_scalar(self.part_u[1], self.top_u, 15, None, ALU.bitwise_and))
                V.done(V.after().tensor_copy(self.part_f[1], self.part_u[1]))
                V.done(V.only(V.mark()).tensor_copy(self.part_f[0], self.part_u[0]))
                iota = row("iota", 16).unsqueeze(1).broadcast_to([128, 16, 16])
                for j in range(2):
                    for k in range(nh):
                        V.done(V.after().tensor_tensor(cand[:, k], self.part_f[j][:, k, :].unsqueeze(2).broadcast_to([128, 16, 16]), iota, ALU.is_equal))
                    between[0]()
                    for k in range(nh):
                        V.done(V.after().tensor_tensor(cand[:, k], cand[:, k], self.best_f[:, k, j, :].unsqueeze(1).broadcast_to([128, 16, 16]), ALU.mult))
                    V.done(V.after().tensor_reduce(self.e_f[j].rearrange("p h a -> p (h a)"), cand.rearrange("p h a b -> p (h a) b"), AX, ALU.add))
                V.done(V.after().scalar_tensor_tensor(self.e_f[0], self.e_f[0], float(NKEYS), self.e_f[1], ALU.mult, ALU.add))
                return V.done(V.after().tensor_copy(idx_out, self.e_f[0]))

        two_heads = Selection(2, 0)

        proj = w(16384, NT, D)

        def project():
            keys_read = T.mark()
            T.after(p_ok)
            for c in range(2):
                hi, lo = next_chunk(last=c == 1)
                for n in range(2):
                    pair = 2 * (pairs[0] % 2)
                    T.after(Mark(evac.sem, pairs[0] - 1))
                    for t in range(NT):
                        for k in range(2):
                            cs = slice((n * 2 + k) * NC, (n * 2 + k + 1) * NC)
                            m = products(ps[:, pair + t, :], (pTh[:, k, t * 128:(t + 1) * 128], pTl[:, k, t * 128:(t + 1) * 128]),
                                         (hi[:, cs], lo[:, cs]), start=(k == 0), stop=(k == 1))
                    m = T.done(m, used if n == 1 else None)
                    pairs[0] += 1
                    for t in range(NT):
                        A.done(A.after(m, keys_read).activation(proj[:, t, (2 * c + n) * NC:(2 * c + n + 1) * NC], ps[:, pair + t, :], ACT.Copy),
                               evac if t else None)

        early = [W[:, 8704:8704 + D], ffn_row]
        chosen = {}
        early_used = []

        def early_gather(r):
            G.eng.wait_ge(chosen[r // 16].sem, chosen[r // 16].value())
            if r >= len(early):
                G.eng.wait_ge(early_used[r - len(early)].sem, early_used[r - len(early)].value())
            G.eng.indirect_dma_start(early[r % len(early)], None, expert_u[:, :],
                                     bass.IndirectOffsetOnAxis(idx[:, 0, r:r + 1], 0)).then_inc(early_in[r % len(early)], 16)

        def early_rows():
            for r in range(len(early)):
                early_gather(r)
            for r in range(EARLY * 16):
                slot = early[r % len(early)]
                m = Mark(early_in[r % len(early)], 16 * (r // len(early) + 1))
                early_used.append(V.done(V.after(m).tensor_tensor_reduce(slot, slot, xn[:, 0, :], 1.0, 0.0, ALU.mult, ALU.add, act[:, 0, r:r + 1])))
                if r + len(early) < EARLY * 16:
                    early_gather(r + len(early))
                yield
        early_row = early_rows()

        def scores_of(n):
            transposes(4, lambda t, k: qb[:, t, k * 128:(k + 1) * 128], to_split(qh, ql), evac.mark())
            A.after(T.mark())
            T.after(V.mark())
            yield
            for t in range(NT):
                T.after(*bank_free[6 + t])
                for k in range(4):
                    s = slice(t * 128, (t + 1) * 128)
                    c = slice((4 * n + k) * 128, (4 * n + k + 1) * 128)
                    m = products(ps[:, 6 + t, k * 128:(k + 1) * 128], (qh[:, k, s], ql[:, k, s]), (KH[:, c], KL[:, c]), start=True, stop=True)
                m = T.done(m)
                dst = s0[n % 2] if t == 0 else s1[:, n * NC:(n + 1) * NC]
                bank_free[6 + t] = [A.done(A.after(m, V.mark()).activation(dst, ps[:, 6 + t, :], ACT.Copy))]
                if t == 0:
                    s0_ok[n] = bank_free[6][0]
            yield

        s0_ok = {}
        for t, _ in enumerate(scores_of(0)):
            V.done(V.after(ffn_in).scalar_tensor_tensor(xn[:, t, :], h[:, t, :], st[:, RSTD + t:RSTD + t + 1], ffn_row, ALU.mult, ALU.mult))
        m = A.done(A.after(p_in).activation(pTh[:, :, :], pTs, ACT.Copy))
        p_ok = V.done(V.after(m).tensor_tensor(pTl[:, :, :], pTs, pTh[:, :, :].bitcast(F32), ALU.subtract))
        for n in range(4):
            scoring = scores_of(n + 1) if n < 3 else iter(())
            steps = iter(SCHEDULE[min(n, 3)])

            def one_step():
                for c in next(steps, ""):
                    if c == "d":
                        tick()
                    elif c == "s":
                        next(scoring)
                    elif c == "p":
                        side_done()
                        project()
                    else:
                        next(early_row, None)
            between[0] = one_step
            hd = 2 * n
            two_heads.keys(s0[n % 2].rearrange("p (h a b) -> p h a b", h=2, a=2), s0_ok[n])
            m = two_heads.experts(idx[:, 0, hd * 16:(hd + 2) * 16].rearrange("p (h a) -> p h a", h=2))
            for k in range(2):
                chosen[hd + k] = m
            V.done(V.after().tensor_copy(gate[:, 0, hd * 16:(hd + 2) * 16], two_heads.top.rearrange("p h a -> p (h a)")))
            assert next(steps, None) is None
        pq_done = [used.mark(), A.mark(), T.mark()]
        for _ in early_row:
            pass
        side_done()
        between[0] = lambda: None
        V.after().nop(nofuse=True).then_inc(rows_used.sem, 2)
        idx_ok = [chosen[5], None]

        xT_rows = over("xT_rows", xT_at, 0, [4, D], F32)
        slots = [xT_rows[:, r, :] for r in range(4)] + [W[:, 4096 + r * D:4096 + (r + 1) * D] for r in range(4)]
        best1, best1_f = W[:, 14336:14592], W[:, 14592:14848]
        G.after(*pq_done)
        G.eng.sem_inc(rows_used.sem, GR - 2)
        V.after(bank_free[6][0], bank_free[7][0])

        def peer_pass(t, table, use, beside, v_per, a_per):
            G.after(idx_ok[t])
            h0 = 0 if t or table is expert_v else EARLY
            lanes = [G, V] + ([A] if a_per else [])
            per = {G.own: 4, V.own: v_per, rows_used: 16}
            if a_per:
                per[A.own] = a_per
            with loop(NH - h0, per, lanes) as i:
                first = rows_used.count - GR
                use(i, h0, None, None, None)
                for j in range(16):
                    r = j % GR
                    free = Mark(rows_used.sem, first + j + 1, 16, i)
                    if j % 4 == 0:
                        ready = G.done(G.after(free).tensor_copy(idx_now[:, j:j + 4], idx[:, t, bass.ds(i * 16 + (h0 * 16 + j), 4)]))
                    for m in (free, ready):
                        G.eng.wait_ge(m.sem, m.value())
                    G.eng.nop(nofuse=True)
                    G.eng.indirect_dma_start(slots[r], None, table[:, :],
                                             bass.IndirectOffsetOnAxis(idx_now[:, j:j + 1], 0)).then_inc(row_in[r], 16)
                    use(i, h0, j, slots[r], Mark(row_in[r], 16 * ((first + j) // GR + 1), 32, i))
                    if beside:
                        beside(i, j)

        def dot(t):
            def f(i, h0, j, r, m):
                if j is None:
                    return
                V.done(V.after(m).tensor_tensor_reduce(junk, r, xn[:, t, :], 1.0, 0.0, ALU.mult, ALU.add, col_now[:, j:j + 1]), rows_used)
                if j == 15:
                    V.done(V.after().tensor_copy(act[:, t, bass.ds(i * 16 + h0 * 16, 16)], col_now[:, :]))
            return f

        def add_row(t):
            def f(i, h0, j, r, m):
                if j is None:
                    V.done(V.after().tensor_copy(col_now[:, :], act[:, t, bass.ds(i * 16 + h0 * 16, 16)]))
                    return
                V.done(V.after(m).scalar_tensor_tensor(h[:, t, :], r, col_now[:, j:j + 1], h[:, t, :], ALU.mult, ALU.add), rows_used)
            return f

        one_head = Selection(1, 256)
        s_now = tmp[:, 0:256].rearrange("p (h a b) -> p h a b", h=1, a=2)
        best_now, best_f_now = (v.rearrange("p h a b -> p (h a b)") for v in (one_head.best, one_head.best_f))

        def keys_of(at, at_best):
            s_ok = A.done(A.after(V.mark()).activation(tmp[:, 0:256], s1[:, at], ACT.Copy))
            m = one_head.keys(s_now, s_ok)
            A.done(A.after(m).activation(best1[:, at_best], best_now, ACT.Copy))
            A.done(A.after(m).activation(best1_f[:, at_best], best_f_now, ACT.Copy))

        def select_keys(i, j):
            if j == 2:
                keys_of(bass.ds(i * 256, 256), bass.ds(i * 32, 32))

        selected = []

        def select_experts(i, j):
            if j == 2:
                A.done(A.after(V.mark()).activation(best_now, best1[:, bass.ds(i * 32, 32)], ACT.Copy))
                m = A.done(A.after().activation(best_f_now, best1_f[:, bass.ds(i * 32, 32)], ACT.Copy))
                V.after(m)
                m = one_head.experts(idx[:, 1, bass.ds(i * 16, 16)].unsqueeze(1))
                selected[:] = [Mark(m.sem, m.const + m.per * (NH - 1))]
                V.done(V.after().tensor_copy(gate[:, 1, bass.ds(i * 16, 16)], one_head.top.rearrange("p h a -> p (h a)")))

        for t in range(NT):
            peer_pass(t, expert_u, dot(t), None if t else select_keys, 1 if t else 12, 0 if t else 3)
            if t == 0:
                for n in range(NH - EARLY, NH):
                    V.after(A.mark())
                    keys_of(slice(n * 256, (n + 1) * 256), slice(n * 32, (n + 1) * 32))
            g3 = heads(gate[:, t, :], NH)
            V.done(V.after().tensor_copy(st[:, 72:80].unsqueeze(2), g3[:, :, 0:1]))
            m = V.done(V.after().tensor_tensor(g3, g3, per_head(st[:, 72:80], NH, 16), ALU.subtract))
            m = A.done(A.after(m).activation(gate[:, t, :], gate[:, t, :], ACT.Exp))
            V.done(V.after(m).tensor_reduce(st[:, 56:64], g3, AX, ALU.add))
            V.done(V.after().reciprocal(st[:, 56:64], st[:, 56:64]))
            V.done(V.after().tensor_tensor(g3, g3, per_head(st[:, 56:64], NH, 16), ALU.mult))
            m = A.done(A.after(V.mark()).activation(act[:, t, :], act[:, t, :], ACT.Gelu_apprx_tanh))
            V.done(V.after(m).tensor_tensor(act[:, t, :], act[:, t, :], gate[:, t, :], ALU.mult))
            peer_pass(t, expert_v, add_row(t), None if t else select_experts, 1 if t else 20, 0 if t else 2)
            idx_ok[1] = selected[0]
        set_junk(rows_used.mark())

        split_next()
        V.done(V.after().tensor_copy(st[:, 95:96], st[:, 0:1]))
        into = stream_entry(COLS["ple"])
        into.part(0, V.mark())
        into.part(1)
        sg = tmp[:, :].rearrange("p (t n) -> p t n", t=NT)

        def add_embeddings(cs):
            def f(banks, got):
                before = V.mark()
                for t in range(NT):
                    m = A.done(A.after(got, before).activation(sg[:, t, :], banks[t], ACT.Sigmoid, scale=st[:, RSTD + t:RSTD + t + 1]),
                               evac if t else None)
                for t in range(NT):
                    V.done(V.after(m).tensor_tensor(sg[:, t, :], sg[:, t, :], proj[:, t, cs], ALU.mult))
                    V.done(V.after().tensor_tensor(h[:, t, cs], h[:, t, cs], sg[:, t, :], ALU.add))
            return f

        after_ple = stream_entry(COLS["norm2"])
        for n in range(4):
            ok = V.mark()
            then = {0: {0: into.later(2), **into.rest()},
                    3: {1: after_ple.later(0, ok), 2: after_ple.later(1, ok), 3: after_ple.later(2, ok)}}.get(n)
            dense(4, add_embeddings(slice(n * NC, (n + 1) * NC)), ready=into.ready if n == 0 else None, then=then)
        into = after_ple
        stream_ok = V.mark()

        B = w(0, NT, 7 * AW)
        V.after(T.mark())

        dense(4, copy_out(lambda t: B[:, t, 0:NC], RSTD), ready=into.ready, then=into.rest(stream_ok))
        dense(4, copy_out(lambda t: B[:, t, NC:2 * NC], RSTD))

        def in2_body(i):
            for j in range(2):
                dense(4, copy_out(lambda t: B[:, t, bass.ds(i * (2 * NC) + (2 + j) * NC, NC)], RSTD))
        dense_loop(3, in2_body, 8, 2, {V.own: 2})
        ok = evac.mark()

        def gating_half():
            for n in range(8, 14):
                yield from dense_steps(4, copy_out(lambda t: B[:, t, n * NC:(n + 1) * NC], RSTD))
        side[0] = gating_half()

        def part2(t, s, n=1):
            return B[:, t, s * AW:(s + n) * AW]
        wsT = W[:, 18432:18432 + AW]
        ws_in = load("ws", wsT, w_spatial_t, V.mark())
        ws_ok = G.done(G.after(ws_in).affine_select(out=heads(wsT, 8), in_=heads(wsT, 8), compare_op=ALU.is_ge, fill=0.0,
                                                    base=0, pattern=[[0, 8], [1, 128]], channel_multiplier=-1))

        def norm_groups(ap, gain, ss, *marks):
            m = A.done(A.after(*marks, *junk_free()).activation(junk[:, 0:AW], ap, ACT.Square))
            m = V.done(V.after(m).tensor_reduce(ss, heads(junk[:, 0:AW], 8), AX, ALU.add))
            set_junk(m)
            rstd(ss, 128)
            V.done(V.after().tensor_tensor(heads(ap, 8), heads(ap, 8), per_head(ss, 8, 128), ALU.mult))
            return V.done(V.after().tensor_tensor(heads(ap, 8), heads(ap, 8), per_dim(row(gain, 128), 8, 128), ALU.mult))

        for t in range(NT):
            norm_groups(part2(t, 0), "q_norm2", st[:, 16:24], ok)
            tick()
            norm_groups(part2(t, 1), "k_norm2", st[:, 24:32])
            tick()
        for t in range(NT):
            silu_ok = A.done(A.after().activation(part2(t, 3), part2(t, 3), ACT.Silu))

        q2T, k2T = W[:, 14336:16384], W[:, 16384:18432]
        ok = V.mark()
        transposes(8, lambda t, k: part2(t, 0)[:, k * 128:(k + 1) * 128], to_plain(q2T), ok)
        transposes(8, lambda t, k: part2(t, 1)[:, k * 128:(k + 1) * 128], to_plain(k2T), ok)
        T.after(A.mark(), V.mark())
        prob2 = [B[:, 0, 0:1024].rearrange("p (k n) -> p k n", k=8), B[:, 1, 0:2048].rearrange("p (k n) -> p k n", k=8)]
        o2 = [part2(0, 0), part2(1, 0)]
        tp = tmp

        def causal_score(t):
            def f(k, o):
                return T.eng.matmul(o, q2T[:, k * S + t * 128:k * S + (t + 1) * 128], k2T[:, k * S:k * S + (t + 1) * 128], start=True, stop=True)
            return f
        V.after(T.mark())
        ok = both_tiles(*[softmax(8, (t + 1) * 128, 128 ** -0.5, t, causal_score(t), 1, prob2[t], st[:, 48 + 8 * t:56 + 8 * t], False, 3)
                          for t in range(NT)])
        pT2 = W[:, 14336:14336 + 3072].rearrange("p (k n) -> p k n", k=8)
        A.after(T.mark())
        V.after(T.mark())
        turn_probabilities(lambda t: prob2[t], lambda k: pT2[:, k, :], ok)
        T.after(A.mark(), V.mark())
        for t in range(NT):
            for g in range(2):
                b = 6 + g
                T.after(*bank_free[b])
                for j in range(4):
                    k = 4 * g + j
                    for kt_ in range(t + 1):
                        at = 0 if t == 0 else 128 + kt_ * 128
                        m = T.eng.matmul(ps[:, b, j * 128:(j + 1) * 128], pT2[:, k, at:at + 128], part2(kt_, 2)[:, k * 128:(k + 1) * 128],
                                         start=(kt_ == 0), stop=(kt_ == t))
                m = T.done(m)
                for j in range(4):
                    k = 4 * g + j
                    s = slice(k * 128, (k + 1) * 128)
                    m2 = V.done(V.after(m, silu_ok).scalar_tensor_tensor(o2[t][:, s], ps[:, b, j * 128:(j + 1) * 128],
                                                                         st[:, 48 + 8 * t + k:49 + 8 * t + k], part2(t, 3)[:, s], ALU.mult, ALU.mult))
                bank_free[b] = [m2]
                tick()
        side_done()
        side_ok = evac.mark()
        aTh, aTl = over("aTh", W_at, 14336, [8, S]), over("aTl", W_at, 16384, [8, S])
        A.after(T.mark())
        transposes(8, lambda t, k: o2[t][:, k * 128:(k + 1) * 128], to_split(aTh, aTl), V.mark())
        T.after(V.mark())

        merged = B[:, :, 2048:4096]
        sTh = over("sTh", W_at, 0, [8, S])
        sTl = over("sTl", W_at, 7 * AW, [8, S])

        def merge_steps(cs, then=None):
            def gated(banks, got):
                before = V.mark()
                for t in range(NT):
                    A.done(A.after(got, before).activation(sg[:, t, :], banks[t], ACT.Sigmoid, scale=st[:, RSTD + t:RSTD + t + 1]),
                           evac if t else None)

            def first(banks, got):
                V.done(V.after(got, evac.mark()).tensor_tensor(merged[:, 0, cs], banks[0], sg[:, 0, :], ALU.mult))
                V.done(V.after().tensor_tensor(merged[:, 1, cs], banks[1], sg[:, 1, :], ALU.mult), evac)
                V.done(V.after().tensor_copy(st[:, 95:96], st[:, 0:1]))

            def second(banks, got):
                V.done(V.after(got, evac.mark()).tensor_tensor(sg[:, 0, :], banks[0], sg[:, 0, :], ALU.mult))
                V.done(V.after().tensor_tensor(sg[:, 1, :], banks[1], sg[:, 1, :], ALU.mult), evac)
                for t in range(NT):
                    V.done(V.after().tensor_tensor(merged[:, t, cs], merged[:, t, cs], sg[:, t, :], ALU.add))
            yield from dense_steps(4, gated)
            yield from dense_steps(2, first, lhs=(aTh, aTl))
            yield from dense_steps(4, gated)
            yield from dense_steps(2, second, lhs=(sTh, sTl), then=then)
        side[0] = merge_steps(slice(0, NC))
        m = V.mark()
        tick()
        for t in range(NT):
            m = A.done(A.after(m, side_ok).activation(part2(t, 4, 2), part2(t, 4, 2), ACT.Gelu_apprx_tanh))
        tick()
        for t in range(NT):
            norm_groups(part2(t, 5), "sgu", st[:, 32:40], m)
            tick()
        T.after(V.mark())
        for t in range(NT):
            zb_ok = A.done(A.after().activation(part2(t, 6), part2(t, 6), ACT.Silu))
        T.after(ws_ok)
        for t in range(NT):
            for g in range(2):
                b = 6 + g
                T.after(*bank_free[b])
                for j in range(4):
                    k = 4 * g + j
                    m = T.eng.matmul(ps[:, b, j * 128:(j + 1) * 128], wsT[:, k * 128:(k + 1) * 128], part2(t, 5)[:, k * 128:(k + 1) * 128],
                                     start=True, stop=True)
                m = T.done(m)
                for j in range(4):
                    k = 4 * g + j
                    s = slice(k * 128, (k + 1) * 128)
                    bs = colv[:, COLS["b_spatial"] + k:COLS["b_spatial"] + k + 1]
                    m2 = V.done(V.after(m).scalar_tensor_tensor(part2(t, 4)[:, s], ps[:, b, j * 128:(j + 1) * 128], bs, part2(t, 4)[:, s], ALU.add, ALU.mult))
                bank_free[b] = [m2]
                tick()
            V.done(V.after(zb_ok).tensor_tensor(part2(t, 4), part2(t, 4), part2(t, 6), ALU.mult))
        A.after(T.mark())
        transposes(8, lambda t, k: part2(t, 4)[:, k * 128:(k + 1) * 128], to_split(sTh, sTl), V.mark())
        T.after(V.mark(), A.mark())

        side_done()
        dense_loop(2, lambda i: [None for _ in merge_steps(bass.ds(i * NC + NC, NC))], 12, 4, {V.own: 5, A.own: 2})
        into = Entry(lambda t, k: merged[:, t, k * 128:(k + 1) * 128])
        ok = V.mark()
        for _ in merge_steps(slice(3 * NC, D), then={0: into.later(0, ok), 1: lambda: (into.part(1, ok), into.part(2))}):
            pass
        merged_ok = V.mark()
        for n in range(4):
            def f(banks, got):
                for t in range(NT):
                    o = h[:, t, n * NC:(n + 1) * NC]
                    m = V.done(V.after(got).tensor_tensor(o, banks[t], o, ALU.add), evac if t else None)
                for t in range(NT):
                    A.after(m).dma_start(out[t * 128:(t + 1) * 128, n * NC:(n + 1) * NC], h[:, t, n * NC:(n + 1) * NC]).then_inc(loads["out"], 16)
            dense(4, f, last=(n == 3), ready=into.ready if n == 0 else None, then={1: into.later(3, merged_ok)} if n == 0 else None)
        assert used.count == CHUNKS == split_at[0]
        nc.scalar.wait_ge(loads["out"], 16 * 4 * NT)


def blocks_of(wt):
    K, N = wt.shape
    return wt.reshape(K // 512, 4, 128, N // NC, NC).transpose(3, 0, 2, 1, 4).reshape(-1, 128, CW)


def kernel(**inputs):
    import concourse.bacc as bacc
    from concourse.bass_utils import run_bass_kernel_spmd

    a = {k: np.asarray(v) for k, v in inputs.items()}
    f32 = np.float32
    a = {k: (v if k in ("x", "positions", "p") else v[0]) for k, v in a.items()}
    w_in, w_in_2 = a["w_in"], a["w_in_2"]
    rope = np.zeros((128, CW), f32)
    rope[:, :DK * QR] = w_in[:, D:].reshape(DK, 128, QR).transpose(1, 0, 2).reshape(128, DK * QR)
    pool = a["w_pool"].reshape(4, 2, 128, 256).transpose(2, 0, 1, 3).reshape(1, 128, CW)
    keys = np.stack([a["sub_k1"], a["sub_k2"]], 1).transpose(3, 0, 1, 2).reshape(1, 128, CW)
    proj = a["w_ple_proj"].reshape(2, 128, 4, NC).transpose(1, 2, 0, 3).reshape(128, 2, CW).transpose(1, 0, 2)
    n = AW
    ga, gb = blocks_of(w_in_2[:, 7 * n:7 * n + D]), blocks_of(w_in_2[:, 7 * n + D:])
    pa, pb = blocks_of(a["w_proj_a_2"]), blocks_of(a["w_proj_b_2"])
    merge = [c for i in range(4) for c in (ga[4 * i:4 * i + 4], pa[2 * i:2 * i + 2], gb[4 * i:4 * i + 4], pb[2 * i:2 * i + 2])]
    weights = np.concatenate([blocks_of(w_in[:, :D]), rope[None], pool, blocks_of(a["w_uq"]), blocks_of(a["w_ukv"]),
                              blocks_of(a["w_out"][:POOL_W]), blocks_of(a["w_out"][POOL_W:]), keys, blocks_of(a["w_pq"]), proj, blocks_of(a["w_ple_gate"]),
                              blocks_of(w_in_2[:, :7 * n])] + merge + [blocks_of(a["w_out_2"])])

    def col(v):
        return v.reshape(-1, 128).T
    cols = np.concatenate([col(a["mix_norm_gain"]), col(a["ffn_norm_gain"]), col(a["ple_norm_gain"]), col(a["norm_g_2"]), col(a["pool_scale"]),
                           col(a["q_lat_gain"]), col(a["kv_lat_gain"]), a["b_spatial_2"].T,
                           col(a["q_norm_gain"][:QN]), col(a["k_norm_gain"][:QN])], 1)
    inv_freq = (f32(10000.0) ** (-np.arange(0, QR, 2, dtype=f32) / f32(QR))).astype(f32)
    rows = np.concatenate([a["q_norm_gain"], a["k_norm_gain"], a["q_norm_g_2"], a["k_norm_g_2"], a["sgu_norm_g_2"],
                           inv_freq, np.arange(16, dtype=f32)])[None]
    pool_op = np.zeros((S, 4, S), f32)
    for g, win in enumerate(POOL_WINDOWS):
        for t in range(S):
            lo = max(0, t - win + 1)
            pool_op[lo:t + 1, g, t] = f32(1) / f32(t + 1 - lo)
            pool_op[t, g, t] -= f32(1)
    arrays = dict(
        x=a["x"][0], cols=cols, rows=rows, positions=a["positions"].reshape(NT, 128).T, ffn_gain=a["ffn_norm_gain"][None],
        pool_op=pool_op.reshape(NT, 128, 4 * S).transpose(1, 0, 2).reshape(128, NT * 4 * S),
        p_t=a["p"][0, 0].T.reshape(2, 128, S).transpose(1, 0, 2).reshape(128, 2 * S),
        w_spatial_t=a["w_spatial_2"].transpose(2, 0, 1).reshape(128, 8 * 128),
        weights=weights, expert_u=a["expert_u"], expert_v=a["expert_v"])
    arrays = {k: np.ascontiguousarray(v) for k, v in arrays.items()}
    nc = bacc.Bacc("TRN2", target_bir_lowering=False, num_devices=1)
    aps = {k: nc.dram_tensor("in_" + k, v.shape, mybir.dt.from_np(v.dtype), kind="ExternalInput").ap() for k, v in arrays.items()}
    out = nc.dram_tensor("out", (S, D), F32, kind="ExternalOutput").ap()
    build(nc, out=out, **aps)
    r = run_bass_kernel_spmd(nc, [{"in_" + k: v for k, v in arrays.items()}], core_ids=[0])
    return r.results[0]["out"].reshape(1, S, D)
```
